# Optimizing a Trainium2 kernel written in Bass

```python
import math
import jax, jax.numpy as jnp
from jax import lax
import numpy as np

D_MODEL = 2048
BATCH = 1
SEQ = 1024
DEPTH = 1

N_MIXERS = 3
EPS = 1e-6
DA_HEADS = 8
DA_QK_DIM = 128
DA_V_DIM = 2 * DA_QK_DIM
DA_WIDTH = DA_HEADS * DA_V_DIM
DA_IN = 4 * DA_HEADS * DA_QK_DIM + 2 * DA_WIDTH
Q_BLOCK = 128
HG_HEADS = 16
HG_KEY_DIM = 128
HG_VAL_DIM = D_MODEL // HG_HEADS
HG_FDIM = HG_HEADS * HG_KEY_DIM
HG_WIDTH = HG_HEADS * HG_VAL_DIM
HG_IN = 2 * HG_FDIM + 2 * HG_WIDTH
HG_CHUNK = 64
CONV_WIDTH = 31
CV_WIDTH = D_MODEL
CV_IN = 3 * CV_WIDTH

kernel_name = "hybrid_diffattn_hgrn2_conformer_adaln"

def _count(kind):
    return len(range(kind, DEPTH, N_MIXERS))

def rmsnorm(x, gain):
    xf = x.astype(jnp.float32)
    y = xf * lax.rsqrt(jnp.mean(xf * xf, axis=-1, keepdims=True) + EPS)
    return (y * gain.astype(jnp.float32)).astype(x.dtype)

def layernorm(x, gain, bias):
    xf = x.astype(jnp.float32)
    mu = jnp.mean(xf, axis=-1, keepdims=True)
    var = jnp.mean(jnp.square(xf - mu), axis=-1, keepdims=True)
    y = (xf - mu) * lax.rsqrt(var + EPS)
    return (y * gain.astype(jnp.float32) + bias.astype(jnp.float32)).astype(x.dtype)

def diff_attention(h, w_in, w_out, lam_q1, lam_k1, lam_q2, lam_k2, subln_g, layer_idx):
    B, S, _ = h.shape
    H, dk, dv = DA_HEADS, DA_QK_DIM, DA_V_DIM
    u = h @ w_in
    q, k, v, gate = jnp.split(u, [2 * H * dk, 4 * H * dk, 4 * H * dk + DA_WIDTH], axis=-1)
    q = q.reshape(B, S, H, 2, dk).transpose(0, 2, 3, 1, 4) * (dk ** -0.5)
    k = k.reshape(B, S, H, 2, dk).transpose(0, 2, 3, 1, 4)
    v = v.reshape(B, S, H, dv).transpose(0, 2, 1, 3)
    lam_init = 0.8 - 0.6 * math.exp(-0.3 * layer_idx)
    lam = (jnp.exp(jnp.sum(lam_q1.astype(jnp.float32) * lam_k1.astype(jnp.float32)))
           - jnp.exp(jnp.sum(lam_q2.astype(jnp.float32) * lam_k2.astype(jnp.float32)))
           + lam_init)
    slopes = 2.0 ** (-8.0 * jnp.arange(1, H + 1, dtype=jnp.float32) / H)
    n_blk = S // Q_BLOCK
    q_blocks = q.reshape(B, H, 2, n_blk, Q_BLOCK, dk).transpose(3, 0, 1, 2, 4, 5)
    key_pos = jnp.arange(S)

    def block(args):
        qb, blk = args
        q_pos = blk * Q_BLOCK + jnp.arange(Q_BLOCK)
        s = jnp.einsum('bhmqd,bhmkd->bhmqk', qb, k).astype(jnp.float32)
        dist = (q_pos[:, None] - key_pos[None, :]).astype(jnp.float32)
        s = s - slopes[None, :, None, None, None] * dist
        s = jnp.where(dist >= 0, s, -jnp.inf)
        p = jax.nn.softmax(s, axis=-1)
        attn = p[:, :, 0] - lam * p[:, :, 1]
        return jnp.einsum('bhqk,bhkd->bhqd', attn.astype(v.dtype), v)

    o = lax.map(block, (q_blocks, jnp.arange(n_blk)))
    o = o.transpose(1, 0, 3, 2, 4).reshape(B, S, H, dv)
    o = rmsnorm(o, subln_g) * (1.0 - lam_init)
    o = o.reshape(B, S, DA_WIDTH) * jax.nn.silu(gate)
    return o @ w_out

def hgrn2(h, w_in, w_out, lb_logits, gnorm_g, layer_idx):
    B, S, _ = h.shape
    H, dk, dv, C = HG_HEADS, HG_KEY_DIM, HG_VAL_DIM, HG_CHUNK
    u = h @ w_in
    q, f, i_in, gate = jnp.split(u, [HG_FDIM, 2 * HG_FDIM, 2 * HG_FDIM + HG_WIDTH], axis=-1)
    lb = jax.nn.softmax(lb_logits.astype(jnp.float32), axis=0)
    lb = (jnp.cumsum(lb, axis=0) - lb[0])[layer_idx]
    f_gate = lb + (1.0 - lb) * jax.nn.sigmoid(f.astype(jnp.float32))
    kk = 1.0 - f_gate
    g = jnp.log(f_gate)
    qf = jax.nn.silu(q.astype(jnp.float32))
    vf = i_in.astype(jnp.float32)
    nC = S // C

    def to_chunks(t, d):
        return t.reshape(B, nC, C, H, d).transpose(1, 0, 3, 2, 4)

    qc, kc, gc, vc = to_chunks(qf, dk), to_chunks(kk, dk), to_chunks(g, dk), to_chunks(vf, dv)
    causal = jnp.tril(jnp.ones((C, C), dtype=bool))

    def step(state, inp):
        q_, k_, g_, v_ = inp
        b = jnp.cumsum(g_, axis=-2)
        diff = b[:, :, :, None, :] - b[:, :, None, :, :]
        decay = jnp.exp(jnp.where(causal[:, :, None], diff, -jnp.inf))
        a = jnp.einsum('bhtd,bhsd,bhtsd->bhts', q_, k_, decay)
        o = jnp.einsum('bhts,bhse->bhte', a, v_) + jnp.einsum('bhtd,bhde->bhte', q_ * jnp.exp(b), state)
        b_last = b[:, :, -1:, :]
        state = (jnp.exp(b_last[:, :, 0, :])[..., None] * state
                 + jnp.einsum('bhsd,bhse->bhde', k_ * jnp.exp(b_last - b), v_))
        return state, o

    s0 = jnp.zeros((B, H, dk, dv), jnp.float32)
    _, o = lax.scan(step, s0, (qc, kc, gc, vc))
    o = o.transpose(1, 0, 3, 2, 4).reshape(B, S, HG_WIDTH).astype(h.dtype)
    o = rmsnorm(o, gnorm_g) * jax.nn.silu(gate)
    return o @ w_out

def conv_module(h, w_in, b_in, dw_kernel, dw_bias, ln_g, ln_b, w_out, b_out):
    u = h @ w_in + b_in
    a, a_gate, gate = jnp.split(u, 3, axis=-1)
    y = a * jax.nn.sigmoid(a_gate)
    y = lax.conv_general_dilated(
        y, dw_kernel[:, None, :].astype(y.dtype), window_strides=(1,),
        padding=[(CONV_WIDTH - 1, 0)], dimension_numbers=('NWC', 'WIO', 'NWC'),
        feature_group_count=CV_WIDTH) + dw_bias
    y = layernorm(y, ln_g, ln_b)
    y = jax.nn.silu(y) * jax.nn.silu(gate)
    return y @ w_out + b_out

def setup_inputs(seed: int = 0) -> dict:
    key = jax.random.key(seed)
    ks = jax.random.split(key, 32)
    D = D_MODEL
    nA, nB, nC = _count(0), _count(1), _count(2)
    nrm = jax.random.normal
    f32 = jnp.float32
    return {
        "x": nrm(ks[0], (BATCH, SEQ, D), f32),
        "c": nrm(ks[1], (BATCH, D), f32),
        "norm_g": 1.0 + 0.02 * nrm(ks[2], (DEPTH, D), f32),
        "ada_w": nrm(ks[3], (DEPTH, D, 3 * D), f32) * D ** -0.5,
        "ada_b": 0.01 * nrm(ks[4], (DEPTH, 3 * D), f32),
        "attn_w_in": nrm(ks[5], (nA, D, DA_IN), f32) * D ** -0.5,
        "attn_w_out": nrm(ks[6], (nA, DA_WIDTH, D), f32) * DA_WIDTH ** -0.5,
        "attn_lam_q1": 0.1 * nrm(ks[7], (nA, DA_QK_DIM), f32),
        "attn_lam_k1": 0.1 * nrm(ks[8], (nA, DA_QK_DIM), f32),
        "attn_lam_q2": 0.1 * nrm(ks[9], (nA, DA_QK_DIM), f32),
        "attn_lam_k2": 0.1 * nrm(ks[10], (nA, DA_QK_DIM), f32),
        "attn_subln_g": 1.0 + 0.02 * nrm(ks[11], (nA, DA_V_DIM), f32),
        "hgrn_w_in": nrm(ks[12], (nB, D, HG_IN), f32) * D ** -0.5,
        "hgrn_w_out": nrm(ks[13], (nB, HG_WIDTH, D), f32) * HG_WIDTH ** -0.5,
        "hgrn_lb_logits": 0.1 * nrm(ks[14], (DEPTH, HG_FDIM), f32),
        "hgrn_gnorm_g": 1.0 + 0.02 * nrm(ks[15], (nB, HG_WIDTH), f32),
        "conv_w_in": nrm(ks[16], (nC, D, CV_IN), f32) * D ** -0.5,
        "conv_b_in": 0.01 * nrm(ks[17], (nC, CV_IN), f32),
        "conv_dw": nrm(ks[18], (nC, CONV_WIDTH, CV_WIDTH), f32) * CONV_WIDTH ** -0.5,
        "conv_dw_b": 0.01 * nrm(ks[19], (nC, CV_WIDTH), f32),
        "conv_ln_g": 1.0 + 0.02 * nrm(ks[20], (nC, CV_WIDTH), f32),
        "conv_ln_b": 0.01 * nrm(ks[21], (nC, CV_WIDTH), f32),
        "conv_w_out": nrm(ks[22], (nC, CV_WIDTH, D), f32) * CV_WIDTH ** -0.5,
        "conv_b_out": 0.01 * nrm(ks[23], (nC, D), f32),
        "final_g": 1.0 + 0.02 * nrm(ks[24], (D,), f32),
    }

def reference(x, c, norm_g, ada_w, ada_b,
              attn_w_in, attn_w_out, attn_lam_q1, attn_lam_k1, attn_lam_q2, attn_lam_k2, attn_subln_g,
              hgrn_w_in, hgrn_w_out, hgrn_lb_logits, hgrn_gnorm_g,
              conv_w_in, conv_b_in, conv_dw, conv_dw_b, conv_ln_g, conv_ln_b, conv_w_out, conv_b_out,
              final_g):
    c_act = jax.nn.silu(c)
    for i in range(DEPTH):
        mod = c_act @ ada_w[i] + ada_b[i]
        shift, scale, gate = jnp.split(mod[:, None, :], 3, axis=-1)
        h = rmsnorm(x, norm_g[i]) * (1.0 + scale) + shift
        kind, j = i % N_MIXERS, i // N_MIXERS
        if kind == 0:
            y = diff_attention(h, attn_w_in[j], attn_w_out[j], attn_lam_q1[j], attn_lam_k1[j],
                               attn_lam_q2[j], attn_lam_k2[j], attn_subln_g[j], i)
        elif kind == 1:
            y = hgrn2(h, hgrn_w_in[j], hgrn_w_out[j], hgrn_lb_logits, hgrn_gnorm_g[j], i)
        else:
            y = conv_module(h, conv_w_in[j], conv_b_in[j], conv_dw[j], conv_dw_b[j],
                            conv_ln_g[j], conv_ln_b[j], conv_w_out[j], conv_b_out[j])
        x = x + gate * y
    return rmsnorm(x, final_g)


_drawn_inputs = setup_inputs


def setup_inputs(seed=0):
    import zlib

    import numpy as np

    out = dict(_drawn_inputs(seed))
    spreads = {}
    factors = {'norm_g': 5.652,
     'ada_b': 5.898,
     'attn_lam_k1': 57.448,
     'attn_lam_q2': 7.001,
     'attn_lam_k2': 4.7,
     'attn_subln_g': 21.613,
     'final_g': 8.586,
     'attn_lam_q1': 8.0}
    for name, (base, spread) in spreads.items():
        noise = np.random.default_rng([zlib.crc32(name.encode()), seed]).standard_normal(out[name].shape)
        drawn = base * np.exp(spread * noise) if base else spread * noise
        out[name] = __import__('jax').numpy.asarray(drawn.astype(out[name].dtype))
    for name, factor in factors.items():
        out[name] = (out[name] * factor).astype(out[name].dtype)
    return out
```

```python
from contextlib import ExitStack
import math

import concourse.bass as bass
from concourse import mybir

F32 = mybir.dt.float32
F32R = mybir.dt.float32r
ALU = mybir.AluOpType
ACT = mybir.ActivationFunctionType

P = 128
D = 2048
S = 1024
KT = D // P
NT = S // P
H = 8
DK = 128
DV = 256
EPS = 1e-6
SCALE = DK ** -0.5
LAM_INIT = 0.8 - 0.6 * math.exp(-0.3 * 0)
MASKED = -1.0e37
HALF = S // 2

CHUNKS = 32
GATE_CHUNK = 24
ADA_PARTS = KT
QUARTERS = 4
PAIR = 2 * P
PAIRS = KT // 2
EARLY = 3
Q_BLOCK0, K_BLOCK0, V_BLOCK0, G_BLOCK0 = 0, 16, 32, 48

ORDER = [7, 6, 5, 4, 3, 2, 1, 0]
OUT_N = 4
NW = D // OUT_N

SBUF_BASE = 16512


def region(nc, start):
    at = [start]

    def put(name, shape, dtype=F32):
        t = nc.alloc_sbuf_tensor_at(name, shape, dtype, offset=at[0])
        size = 4
        for n in shape[1:]:
            size *= n
        at[0] += (size + 31) // 32 * 32
        return t

    return put, at


def after(eng, sem, count):
    if isinstance(count, int) and count <= 0:
        return
    eng.wait_ge(sem, count)


def after_apart(eng, waits, held):
    for (_, count), register in zip(waits, held):
        if not isinstance(count, int):
            eng.reg_mov(register, count)
    if not isinstance(waits[0][1], int):
        eng.wait_ge(waits[0][0], 1)
    for (sem, count), register in zip(waits, held):
        after(eng, sem, count if isinstance(count, int) else register)


def place_weights(nc, t):
    put, at = region(nc, t.free_at)
    t.w_raw = put("w_raw", [P, KT, 2 * P])
    t.w_hi = [put(f"w_hi{i}", [P, KT, P], F32R) for i in range(2)]
    t.w_lo = [put(f"w_lo{i}", [P, KT, P], F32R) for i in range(2)]
    return at[0]


def modulation_and_first_blocks(nc, sem, t, A):
    w_raw, w_hi, w_lo = t.w_raw, t.w_hi, t.w_lo
    put, _ = region(nc, t.lo_at)
    xt = [put(f"x_tile{i}", [P, D]) for i in range(NT)]
    put, at = region(nc, t.free_at)
    ada = [put(f"ada_piece{i}", [P, ADA_PARTS // QUARTERS, 2, PAIR]) for i in range(QUARTERS)]
    h = put("h", [P, 2, S])
    junk = nc.alloc_sbuf_tensor_at("squares", [P, D], F32, offset=at[0] - 4 * D)
    put, at = region(nc, t.after_w)
    we_raw = [put(f"early_w_raw{j}", [P, EARLY * P]) for j in range(2)]
    we_hi = [put(f"early_w_hi{j}", [P, EARLY * P], F32R) for j in range(2)]
    we_lo = [put(f"early_w_lo{j}", [P, EARLY * P], F32R) for j in range(2)]
    acc = [put(f"ada_sum{i}", [P, 2, PAIR]) for i in range(2)]
    vec_rows = put("vector_rows", [70, P])
    c_col = put("c_col", [P, KT])
    c_exp = put("c_exp", [P, KT])
    vec_cols = put("vector_cols", [P, 70])
    x_ssq = put("x_ssq", [P, NT])
    x_rstd = put("x_rstd", [P, NT])
    lam_prod = put("lam_prod", [P, 2])
    lam_exp = put("lam_exp", [P, 2])
    mod_cols = put("mod_cols", [P, 2, KT])
    gain_cols = put("gain_cols", [P, KT])
    assert at[0] <= nc.sbuf_usable_end

    small_loaded, x_loaded = sem("small_loaded"), [sem(f"x_loaded{m}") for m in range(NT)]
    ada_loaded = [sem(f"ada_loaded{s}") for s in range(QUARTERS)]
    we_loaded, w_loaded = [sem(f"early_w_loaded{j}") for j in range(2)], sem("w_first_loaded")
    ones_set, ident_zero, ident_set = sem("ones_set"), sem("ident_zero"), sem("ident_set")
    c_step, c_exp_ready, c_ready = sem("c_step"), sem("c_exp_ready"), sem("c_ready")
    ssq_ready, ms_ready, rstd_ready, x_scaled = sem("ssq_ready"), sem("ms_ready"), sem("rstd_ready"), sem("x_scaled")
    xT_ready, xT_by_act, xT_by_dve = sem("xT_ready"), sem("xT_taken_by_act"), sem("xT_taken_by_dve")
    vec_ready, vec_taken, lam_prod_ready, lam_sum_ready = sem("vec_ready"), sem("vec_taken"), sem("lam_prod_ready"), sem("lam_sum_ready")
    lam_exp_ready = sem("lam_exp_ready")
    ada_summed, ada_multiplied, mod_ready, mod_added, gain_ready = sem("ada_summed"), sem("ada_multiplied"), sem("mod_ready"), sem("mod_added"), sem("gain_ready")
    h_ready, h_hi_ready, h_lo_ready = sem("h_ready"), sem("h_hi_ready"), sem("h_lo_ready")
    we_hi_ready, we_lo_ready, pair_done = sem("early_w_hi_ready"), sem("early_w_lo_ready"), sem("early_products")

    ROWS = ADA_PARTS // QUARTERS
    SUMS = (ROWS - 1) * QUARTERS

    def xT_ps(n):
        bank = t.early_ps[n % 6 // 2]
        return bank[:, n % 2 * 512:(n % 2 + 1) * 512]

    vec_ps = t.late_ps[:, 0:512]
    mod_ps = t.late_ps[:, 512:516].rearrange("p (m k) -> p m k", m=2)

    def pairs(body):
        for q in range(PAIRS + 1):
            body(q, q % 2)

    def is_pair(q):
        return q < PAIRS

    def has_last(q, back=1):
        return q >= back

    block = ExitStack()
    with block as ctx:
        block = ctx.enter_context(nc.Block())

        @block.sync
        def _(sp):
            sp.dma_start(c_col[:], A["c"][0].rearrange("(p t) -> p t", t=KT)).then_inc(small_loaded, 16)
            rows = A["ada_b"][0].rearrange("(j p) -> j p", p=P)
            sp.dma_start(vec_rows[0:48, :], rows).then_inc(small_loaded, 16)
            sp.dma_start(vec_rows[48:64, :], A["norm_g"][0].rearrange("(j p) -> j p", p=P)).then_inc(small_loaded, 16)
            sp.dma_start(vec_rows[64:66, :], A["attn_subln_g"][0].rearrange("(j p) -> j p", p=P)).then_inc(small_loaded, 16)
            for j, name in enumerate(("attn_lam_q1", "attn_lam_k1", "attn_lam_q2", "attn_lam_k2")):
                sp.dma_start(vec_rows[66 + j:67 + j, :], A[name]).then_inc(small_loaded, 16)
            for m in range(NT):
                sp.dma_start(xt[m][:], A["x"][0, m * P:(m + 1) * P, :]).then_inc(x_loaded[m], 16)
            ada_rows = A["ada_w"][0].rearrange("(p t) (m n) -> p t m n", t=ADA_PARTS, m=3)

            def load_we(q, j):
                after(sp, we_hi_ready, 2 * (q - 1) + j + 1 if has_last(q) else 0)
                after(sp, we_lo_ready, 2 * (q - 1) + j + 1 if has_last(q) else 0)
                sp.dma_start(we_raw[j][:], A["attn_w_in"][0][q * PAIR + j * P:q * PAIR + (j + 1) * P, 0:EARLY * P]).then_inc(we_loaded[j], 16)

            def body(q, par):
                for s in range(QUARTERS):
                    if s % 2 == 0 and has_last(q):
                        load_we(q - 1, s // 2)
                    if is_pair(q):
                        if has_last(q):
                            sp.wait_ge(ada_summed, SUMS * (q - 1) + (ROWS - 1) * (s + 1))
                            sp.wait_ge(ada_multiplied, QUARTERS * (q - 1) + s + 1)
                        for m in range(2):
                            sp.dma_start(ada[s][:, :, m, :], ada_rows[:, s * ROWS:(s + 1) * ROWS, m, q * PAIR:(q + 1) * PAIR]).then_inc(ada_loaded[s], 16)

            pairs(body)
            sp.wait_ge(ada_summed, SUMS * (PAIRS - 1) + (ROWS - 1) * 2)
            sp.wait_ge(ada_multiplied, QUARTERS * (PAIRS - 1) + 2)
            sp.dma_start(w_raw[:, :, P:2 * P], A["attn_w_in"][0][:, EARLY * P:(EARLY + 1) * P].rearrange("(k p) n -> p k n", p=P)).then_inc(w_loaded, 16)

        @block.gpsimd
        def _(pool):
            nc.gpsimd.memset(t.ident[:], 0.0).then_inc(ident_zero, 1)
            pool.wait_ge(ident_zero, 1)
            nc.gpsimd.affine_select(out=t.ident[:], in_=t.ident[:], compare_op=ALU.not_equal, fill=1.0, base=0,
                                    pattern=[[-1, P]], channel_multiplier=1).then_inc(ident_set, 1)
            nc.gpsimd.memset(t.ones[:], 1.0).then_inc(ones_set, 1)
            nc.gpsimd.memset(t.minus_half[:], -0.5).then_inc(ones_set, 1)
            pool.wait_ge(ones_set, 2)
            for m in range(NT):
                pool.wait_ge(ssq_ready, m + 1)
                nc.gpsimd.tensor_scalar(x_ssq[:, m:m + 1], x_ssq[:, m:m + 1], 1.0 / D, EPS, ALU.mult, ALU.add).then_inc(ms_ready, 1)
                pool.wait_ge(ms_ready, m + 1)
                nc.gpsimd.tensor_tensor(x_rstd[:, m:m + 1], x_ssq[:, m:m + 1], t.minus_half[:, 0:1], ALU.pow).then_inc(rstd_ready, 1)

            def body(q, par):
                if not has_last(q):
                    return
                for j in range(2):
                    pool.wait_ge(we_hi_ready, 2 * (q - 1) + j + 1)
                    nc.gpsimd.tensor_tensor(we_lo[j][:], we_raw[j][:], we_hi[j][:].bitcast(F32), ALU.subtract).then_inc(we_lo_ready, 1)

            pairs(body)

        @block.scalar
        def _(act):
            act.wait_ge(small_loaded, 128)
            nc.scalar.activation(c_exp[:], c_col[:], ACT.Exp, scale=-1.0).then_inc(c_exp_ready, 1)

            def square(m):
                act.wait_ge(x_loaded[m], 16)
                after(act, ssq_ready, m)
                nc.scalar.activation(junk[:], xt[m][:], ACT.Square, accum_out=x_ssq[:, m:m + 1]).then_inc(ssq_ready, 1)

            def take(m):
                for g in range(2):
                    n = 4 * m + g
                    act.wait_ge(xT_ready, n + 1)
                    nc.scalar.activation(t.xT[:, 4 * g:4 * g + 4, m * P:(m + 1) * P], xT_ps(n).rearrange("p (k s) -> p k s", k=4),
                                         ACT.Copy).then_inc(xT_by_act, 1)

            for m in range(NT):
                square(m)
                if m == 0:
                    act.wait_ge(lam_sum_ready, 1)
                    nc.scalar.activation(lam_exp[:], vec_ps[:, 96:98], ACT.Exp).then_inc(lam_exp_ready, 1)
                if m > 0:
                    take(m - 1)
            take(NT - 1)

            def body(q, par):
                if not has_last(q):
                    return
                if q == 1:
                    act.wait_ge(xT_by_act, 2 * NT)
                    act.wait_ge(xT_by_dve, 2 * NT)
                    act.wait_ge(ssq_ready, NT)

                def split(j):
                    act.wait_ge(we_loaded[j], 16 * q)
                    if has_last(q, 2):
                        act.wait_ge(pair_done, 2 * (q - 2) + j + 1)
                    nc.scalar.activation(we_hi[j][:], we_raw[j][:], ACT.Copy).then_inc(we_hi_ready, 1)

                split(0)
                for j in range(2):
                    if j == 0:
                        act.wait_ge(gain_ready, q)
                    if has_last(q, 2):
                        act.wait_ge(h_lo_ready, 2 * (q - 2) + j + 1)
                    k = 2 * (q - 1) + j
                    nc.scalar.activation(h[:, j, :], t.xT[:, k, :], ACT.Identity,
                                         bias=mod_cols[:, 0, k:k + 1], scale=gain_cols[:, k:k + 1]).then_inc(h_ready, 1)
                    act.wait_ge(h_ready, k + 1)
                    nc.scalar.activation(t.h_hi[:, k, :], h[:, j, :], ACT.Copy).then_inc(h_hi_ready, 1)
                split(1)

            pairs(body)
            act.wait_ge(w_loaded, 16)
            act.wait_ge(ada_summed, SUMS * PAIRS)
            act.wait_ge(ada_multiplied, QUARTERS * PAIRS)
            nc.scalar.activation(w_hi[1][:], w_raw[:, :, P:2 * P], ACT.Copy).then_inc(t.w_hi_ready, 1)

        @block.vector
        def _(dve):
            dve.wait_ge(c_exp_ready, 1)
            nc.vector.tensor_scalar_add(c_exp[:], c_exp[:], 1.0).then_inc(c_step, 1)
            dve.wait_ge(c_step, 1)
            nc.vector.reciprocal(c_exp[:], c_exp[:]).then_inc(c_step, 1)
            dve.wait_ge(c_step, 2)
            nc.vector.tensor_tensor(t.c_act[:], c_col[:], c_exp[:], ALU.mult).then_inc(c_ready, 1)
            dve.wait_ge(vec_ready, 1)
            nc.vector.tensor_copy(vec_cols[:], vec_ps[:, 0:70]).then_inc(vec_taken, 1)
            dve.wait_ge(vec_taken, 1)
            nc.vector.tensor_tensor(lam_prod[:], vec_cols[:, 66:70:2], vec_cols[:, 67:70:2], ALU.mult).then_inc(lam_prod_ready, 1)
            nc.vector.tensor_scalar(t.subln_col[:], vec_cols[:, 64:66], 1.0 - LAM_INIT, None, ALU.mult)

            def scale(m):
                dve.wait_ge(rstd_ready, m + 1)
                nc.vector.tensor_scalar(xt[m][:], xt[m][:], x_rstd[:, m:m + 1], None, ALU.mult).then_inc(x_scaled, 1)

            def take(m):
                for g in range(2, 4):
                    n = 4 * m + g
                    dve.wait_ge(xT_ready, n + 1)
                    nc.vector.tensor_copy(t.xT[:, 4 * g:4 * g + 4, m * P:(m + 1) * P],
                                          xT_ps(n).rearrange("p (k s) -> p k s", k=4)).then_inc(xT_by_dve, 1)

            def piece(q, par, s):
                dve.wait_ge(ada_loaded[s], 32 * (q + 1))
                for r in range(ROWS - 1):
                    n = (ROWS - 1) * s + r
                    c = t.c_act[:, s * ROWS + r:s * ROWS + r + 1]
                    if n == 0:
                        if has_last(q, 2):
                            dve.wait_ge(mod_ready, q - 1)
                        nc.vector.tensor_scalar(acc[par][:], ada[s][:, r], c, None, ALU.mult).then_inc(ada_summed, 1)
                    else:
                        dve.wait_ge(ada_summed, SUMS * q + n)
                        nc.vector.scalar_tensor_tensor(out=acc[par][:], in0=ada[s][:, r], scalar=c, in1=acc[par][:],
                                                       op0=ALU.mult, op1=ALU.add).then_inc(ada_summed, 1)

            for m in range(NT):
                scale(m)
                if m > 0:
                    take(m - 1)
            dve.wait_ge(c_ready, 1)
            piece(0, 0, 0)
            take(NT - 1)
            dve.wait_ge(lam_exp_ready, 1)
            nc.vector.scalar_tensor_tensor(out=t.neg_lam[:], in0=lam_exp[:, 1:2], scalar=-LAM_INIT, in1=lam_exp[:, 0:1],
                                           op0=ALU.add, op1=ALU.subtract)

            def columns(q):
                two = slice(2 * (q - 1), 2 * q)
                biases = vec_cols[:, 0:2 * KT].rearrange("p (m k) -> p m k", m=2)
                dve.wait_ge(mod_ready, q)
                nc.vector.tensor_tensor(mod_cols[:, :, two], mod_ps, biases[:, :, two], ALU.add).then_inc(mod_added, 1)
                dve.wait_ge(mod_added, q)
                nc.vector.scalar_tensor_tensor(out=gain_cols[:, two], in0=mod_cols[:, 1, two], scalar=1.0,
                                               in1=vec_cols[:, 48:64][:, two], op0=ALU.add, op1=ALU.mult).then_inc(gain_ready, 1)

            def h_lo(q, j):
                k = 2 * (q - 1) + j
                dve.wait_ge(h_hi_ready, k + 1)
                nc.vector.tensor_tensor(t.h_lo[:, k, :], h[:, j, :],
                                        t.h_hi[:, k, :].bitcast(F32), ALU.subtract).then_inc(h_lo_ready, 1)

            def body(q, par):
                if not has_last(q):
                    for s in range(1, QUARTERS):
                        piece(q, par, s)
                    dve.wait_ge(xT_ready, 4 * NT)
                    return
                if is_pair(q):
                    piece(q, par, 0)
                columns(q)
                if is_pair(q):
                    piece(q, par, 1)
                h_lo(q, 0)
                if is_pair(q):
                    piece(q, par, 2)
                h_lo(q, 1)
                if is_pair(q):
                    piece(q, par, 3)

            pairs(body)
            dve.wait_ge(t.w_hi_ready, 1)
            nc.vector.tensor_tensor(w_lo[1][:], w_raw[:, :, P:2 * P], w_hi[1][:].bitcast(F32), ALU.subtract).then_inc(t.w_lo_ready, 1)

        @block.tensor
        def _(pe):
            pe.wait_ge(ident_set, 1)
            pe.wait_ge(ones_set, 2)
            pe.wait_ge(small_loaded, 128)
            nc.tensor.transpose(vec_ps[:, 0:70], vec_rows[:], t.ident[0:70, 0:70]).then_inc(vec_ready, 1)
            pe.wait_ge(lam_prod_ready, 1)
            nc.tensor.matmul(vec_ps[:, 96:98], t.ones[:], lam_prod[:], start=True, stop=True).then_inc(lam_sum_ready, 1)
            for m in range(NT):
                pe.wait_ge(x_scaled, m + 1)
                for g in range(4):
                    after(pe, xT_by_dve if g < 2 else xT_by_act, 2 * (m - 2) + g + 1 if g < 2 else 2 * (m - 1) + g - 1)
                    for j in range(4):
                        k = 4 * g + j
                        last = nc.tensor.transpose(xT_ps(4 * m + g)[:, j * P:(j + 1) * P], xt[m][:, k * P:(k + 1) * P], t.ident[:])
                    last.then_inc(xT_ready, 1)

            def multiply(q, s):
                if s == 0:
                    if has_last(q):
                        pe.wait_ge(mod_added, q)
                    else:
                        pe.wait_ge(c_ready, 1)
                pe.wait_ge(ada_loaded[s], 32 * (q + 1))
                row = ROWS - 1
                for m in range(2):
                    for j in range(2):
                        last = nc.tensor.matmul(mod_ps[:, m, j:j + 1], ada[s][:, row, m, j * P:(j + 1) * P],
                                                t.c_act[:, s * ROWS + row:s * ROWS + row + 1], start=(s == 0 and m == 0 and j == 0), stop=False)
                last.then_inc(ada_multiplied, 1)

            def add_partitions(q, par):
                pe.wait_ge(ada_summed, SUMS * (q + 1))
                for m in range(2):
                    for j in range(2):
                        last = nc.tensor.matmul(mod_ps[:, m, j:j + 1], acc[par][:, m, j * P:(j + 1) * P], t.ones[:, 0:1], start=False,
                                                stop=(m == 1 and j == 1))
                last.then_inc(mod_ready, 1)

            def products(q, j):
                k = 2 * q + j
                first = k == 0
                if first:
                    pe.wait_ge(xT_by_act, 2 * NT)
                    pe.wait_ge(xT_by_dve, 2 * NT)
                pe.wait_ge(h_lo_ready, k + 1)
                pe.wait_ge(we_lo_ready, k + 1)
                last_k = k == KT - 1
                for b in range(EARLY):
                    for i, (w, h) in enumerate(((we_hi, t.h_hi), (we_hi, t.h_lo), (we_lo, t.h_hi))):
                        for half in range(2):
                            cols = slice(half * HALF, (half + 1) * HALF)
                            last = nc.tensor.matmul(t.early_ps[b][:, cols], w[j][:, b * P:(b + 1) * P],
                                                    h[:, k, cols], start=(first and i == 0), stop=(last_k and i == 2))
                    if last_k:
                        last.then_inc(t.proj_ready, 1)
                if not last_k:
                    last.then_inc(pair_done, 1)

            def body(q, par):
                if has_last(q, 2):
                    products(q - 2, 1)
                if is_pair(q):
                    multiply(q, 0)
                    multiply(q, 1)
                if has_last(q):
                    products(q - 1, 0)
                if is_pair(q):
                    multiply(q, 2)
                    multiply(q, 3)
                    add_partitions(q, par)
                else:
                    products(q - 1, 1)

            pairs(body)


def input_projection(nc, sem, t, A, u_dram):
    w_raw, w_hi, w_lo = t.w_raw, t.w_hi, t.w_lo
    put, at = region(nc, t.after_w)
    u_out = [put(f"u_out{i}", [P, S]) for i in range(2)]
    sig = put("sigmoid", [P, S])
    ada_gate = put("ada_gate_rows", [P, D])
    assert at[0] <= nc.sbuf_usable_end
    u_ps = [t.early_ps[0], t.late_ps]

    w_loaded, w_hi_ready, w_lo_ready = sem("w_loaded"), t.w_hi_ready, t.w_lo_ready
    proj_ready, proj_taken, u_free = t.proj_ready, sem("proj_taken"), [sem(f"u_stored{i}") for i in range(2)]
    gate_exp_ready, silu_step, silu_ready = sem("gate_exp_ready"), sem("silu_step"), sem("silu_ready")
    acc_zero, acc_row_loaded, ada_gate_loaded, gate_summed = sem("gate_acc_zero"), sem("gate_bias_loaded"), sem("ada_gate_loaded"), sem("gate_summed")
    C0 = 2
    C_ROWS = C0 + ADA_PARTS // 2

    ctx = ExitStack()
    with ctx:
        block = ctx.enter_context(nc.Block())

        @block.sync
        def _(sp):
            def load(c):
                sp.wait_ge(w_hi_ready, 2 * c - EARLY)
                sp.wait_ge(w_lo_ready, 2 * c - EARLY)
                sp.dma_start(w_raw[:], A["attn_w_in"][0][:, bass.ds(c * 2 * P, 2 * P)].rearrange("(k p) n -> p k n", p=P)).then_inc(w_loaded, 16)

            def load_gate_rows(c, b):
                r = 2 * (c - C0) + b
                after(sp, gate_summed, r)
                rows = A["ada_w"][0].rearrange("(p t) n -> p t n", t=ADA_PARTS)
                sp.dma_start(ada_gate[:], rows[:, bass.ds(r, 1), 2 * D:3 * D].rearrange("p o n -> p (o n)")).then_inc(ada_gate_loaded, 16)

            def store(c, b, gate=False):
                if gate:
                    sp.wait_ge(silu_ready, 2 * c + b - 2 * GATE_CHUNK + 1)
                else:
                    sp.wait_ge(proj_taken, 2 * c + b + 1)
                sp.dma_start(u_dram[bass.ds(2 * c + b, 1)].rearrange("o p s -> p (o s)"), u_out[b][:]).then_inc(u_free[b], 16)

            def chunk(c, gate=False, rows=False, more=True):
                if rows:
                    load_gate_rows(c, 0)
                if more:
                    load(c + 1)
                store(c, 0, gate)
                if rows:
                    load_gate_rows(c, 1)
                store(c, 1, gate)

            load(C0)
            for n in range(EARLY):
                store(n // 2, n % 2)
            sp.wait_ge(acc_zero, 1)
            sp.dma_start(t.gate_acc[0:1, :], A["ada_b"][:, 2 * D:3 * D]).then_inc(acc_row_loaded, 16)
            store(1, 1)
            chunk(C0, rows=True)
            with sp.Fori(C0 + 1, C_ROWS) as c:
                chunk(c, rows=True)
            with sp.Fori(C_ROWS, GATE_CHUNK) as c:
                chunk(c)
            with sp.Fori(GATE_CHUNK, CHUNKS - 1) as c:
                chunk(c, gate=True)
            chunk(CHUNKS - 1, gate=True, more=False)
            for b in range(2):
                sp.wait_ge(u_free[b], 16 * CHUNKS)

        @block.scalar
        def _(act):
            def split_hi(c, b):
                act.wait_ge(w_loaded, 16 * (c - C0 + 1))
                act.wait_ge(proj_ready, 2 * c + b - 1)
                nc.scalar.activation(w_hi[b][:], w_raw[:, :, b * P:(b + 1) * P], ACT.Copy).then_inc(w_hi_ready, 1)

            def take(c, b, gate=False, banks=None):
                act.wait_ge(proj_ready, 2 * c + b + 1)
                after(act, u_free[b], 16 * c)
                if gate:
                    after(act, silu_ready, 2 * c + b - 2 * GATE_CHUNK)
                    nc.scalar.activation(sig[:], u_ps[b][:], ACT.Exp, scale=-1.0).then_inc(gate_exp_ready, 1)
                nc.scalar.activation(u_out[b][:], (banks or u_ps[b])[:], ACT.Copy).then_inc(proj_taken, 1)

            def chunk(c, gate=False, more=True):
                split_hi(c, 1)
                take(c, 0, gate)
                if more:
                    split_hi(c + 1, 0)
                take(c, 1, gate)

            for n in range(EARLY):
                take(n // 2, n % 2, banks=t.early_ps[n])
            split_hi(C0, 0)
            take(1, 1)
            with act.Fori(C0, GATE_CHUNK) as c:
                chunk(c)
            chunk(GATE_CHUNK, gate=True)
            with act.Fori(GATE_CHUNK + 1, CHUNKS - 1) as c:
                chunk(c, gate=True)
            chunk(CHUNKS - 1, gate=True, more=False)

        @block.vector
        def _(dve):
            def split_lo(c, b):
                dve.wait_ge(w_hi_ready, 2 * c + b - EARLY + 1)
                nc.vector.tensor_tensor(w_lo[b][:], w_raw[:, :, b * P:(b + 1) * P], w_hi[b][:].bitcast(F32), ALU.subtract).then_inc(w_lo_ready, 1)

            def sum_gate(c, b):
                r = 2 * (c - C0) + b
                dve.wait_ge(ada_gate_loaded, 16 * (r + 1))
                after(dve, gate_summed, r)
                nc.vector.scalar_tensor_tensor(out=t.gate_acc[:], in0=ada_gate[:], scalar=t.c_act[:, bass.ds(r, 1)], in1=t.gate_acc[:],
                                               op0=ALU.mult, op1=ALU.add).then_inc(gate_summed, 1)

            def silu(c, b):
                n = 2 * c + b - 2 * GATE_CHUNK
                dve.wait_ge(gate_exp_ready, n + 1)
                nc.vector.tensor_scalar_add(sig[:], sig[:], 1.0).then_inc(silu_step, 1)
                dve.wait_ge(silu_step, 2 * n + 1)
                nc.vector.reciprocal(sig[:], sig[:]).then_inc(silu_step, 1)
                dve.wait_ge(silu_step, 2 * n + 2)
                dve.wait_ge(proj_taken, 2 * c + b + 1)
                nc.vector.tensor_tensor(u_out[b][:], u_out[b][:], sig[:], ALU.mult).then_inc(silu_ready, 1)

            def chunk(c, rows=False, gate=False, more=True):
                split_lo(c, 1)
                if rows:
                    sum_gate(c, 0)
                if gate:
                    silu(c, 0)
                if more:
                    split_lo(c + 1, 0)
                if rows:
                    sum_gate(c, 1)
                if gate:
                    silu(c, 1)

            nc.vector.memset(t.gate_acc[:], 0.0).then_inc(acc_zero, 1)
            split_lo(C0, 0)
            dve.wait_ge(acc_row_loaded, 16)
            chunk(C0, rows=True)
            with dve.Fori(C0 + 1, C_ROWS) as c:
                chunk(c, rows=True)
            with dve.Fori(C_ROWS, GATE_CHUNK) as c:
                chunk(c)
            with dve.Fori(GATE_CHUNK, CHUNKS - 1) as c:
                chunk(c, gate=True)
            chunk(CHUNKS - 1, gate=True, more=False)

        @block.tensor
        def _(pe):
            def product(c, b):
                pe.wait_ge(w_lo_ready, 2 * c + b - EARLY + 1)
                if not isinstance(c, int):
                    pe.wait_ge(proj_taken, 2 * c + b - 1)
                for k in range(KT):
                    for j, (w, h) in enumerate(((w_hi, t.h_hi), (w_hi, t.h_lo), (w_lo, t.h_hi))):
                        for half in range(2):
                            cols = slice(half * HALF, (half + 1) * HALF)
                            last = nc.tensor.matmul(u_ps[b][:, cols], w[b][:, k, :], h[:, k, cols],
                                                    start=(k == 0 and j == 0), stop=(k == KT - 1 and j == 2))
                last.then_inc(proj_ready, 1)

            product(1, 1)
            with pe.Fori(C0, CHUNKS) as c:
                product(c, 0)
                product(c, 1)


def attention(nc, sem, t, u_dram, og_dram):
    put, at = region(nc, t.hi_at)
    qk_raw = put("qk_raw", [P, 4, S])
    v_raw = put("v_raw", [P, 2, S])
    gate = put("gate_T", [P, 2, S])
    qk_hi = [put(f"qk_hi{i}", [P, 4, S], F32R) for i in range(2)]
    qk_lo = [put(f"qk_lo{i}", [P, 4, S], F32R) for i in range(2)]
    v_hi = [put(f"v_hi{i}", [P, NT, DV], F32R) for i in range(2)]
    v_lo = [put(f"v_lo{i}", [P, NT, DV], F32R) for i in range(2)]
    e = [[put(f"e{i}{m}", [P, S]) for m in range(2)] for i in range(2)]
    a = [put(f"a{i}", [P, S]) for i in range(2)]
    aT_hi = [put(f"aT_hi{i}", [P, S], F32R) for i in range(2)]
    aT_lo = [put(f"aT_lo{i}", [P, S], F32R) for i in range(2)]
    o = [put(f"o{i}", [P, NT, DV]) for i in range(2)]
    og_out = [put(f"og_out{i}", [P, 4 * P]) for i in range(2)]
    bias = [put(f"alibi{i}", [P, S]) for i in range(2)]
    junk = put("o_squares", [P, DV])
    row_min = [put(f"row_min{i}", [P, 2]) for i in range(2)]
    row_sum = [put(f"row_sum{i}", [P, 2]) for i in range(2)]
    row_inv = [put(f"row_inv{i}", [P, NT, 2]) for i in range(2)]
    ratio = put("ratio", [P, 1])
    o_ssq = [put(f"o_ssq{i}", [P, NT]) for i in range(2)]
    o_rstd = put("o_rstd", [P, NT])
    one_in_dv = put("one_in_dv", [P, NT])
    eps = put("eps", [P, NT])
    assert at[0] <= nc.sbuf_usable_end

    V_STEPS = {2: (0,), 3: (1,), 4: (2,), 5: (3,)}
    OG_STEPS = {5: (0,), 6: (1,), 7: (2, 3)}

    def groups_of(s, first=False, has_next=True, has_tiles=True):
        found = []
        tile = s - 2
        if tile >= 0 and has_tiles or tile < 0 and not first:
            i = ORDER[tile % NT]
            found += [("a", tile, g) for g in range(i // 4 + 1)]
        if has_next:
            found += [("v", s, g) for g in V_STEPS.get(s, ())]
        if not first:
            found += [("og", s, g) for g in OG_STEPS.get(s, ())]
        return found

    def listed(**kinds):
        return [g for s in range(NT) for g in groups_of(s, **kinds)]

    PROLOGUE = [("v", -1, g) for g in range(4)]
    FIRST, STEADY = listed(first=True), listed()
    LAST = listed(has_next=False)

    def split_ones(groups):
        return [g for g in groups if g[0] != "og"]

    def made(h, groups, place):
        if isinstance(h, int) and h < 0:
            return place
        if isinstance(h, int) and h == 0:
            return len(PROLOGUE) + place
        short = len(STEADY) - len(LAST) if isinstance(h, int) and h == H else 0
        return (h - 1) * len(STEADY) + (len(PROLOGUE) + len(FIRST) + place - short)

    def split(h, groups, place):
        here = len(split_ones(groups[:place]))
        if isinstance(h, int) and h < 0:
            return here
        if isinstance(h, int) and h == 0:
            return len(PROLOGUE) + here
        short = len(STEADY) - len(LAST) if isinstance(h, int) and h == H else 0
        return (h - 1) * len(split_ones(STEADY)) + (len(PROLOGUE) + len(split_ones(FIRST)) + here - short)

    def bank_of(h, place):
        if isinstance(h, int) and h < 0:
            return place % 2
        if isinstance(h, int) and h == 0:
            return (len(PROLOGUE) + place) % 2
        return (len(PROLOGUE) + len(FIRST) + place) % 2

    assert len(STEADY) % 2 == 0

    def window_groups(h):
        if isinstance(h, int):
            if h < 0:
                return PROLOGUE
            if h == 0:
                return FIRST
            if h == H - 1:
                return LAST
            if h == H:
                return [g for s in range(NT) for g in groups_of(s, has_next=False, has_tiles=False)]
        return STEADY

    def groups_at(h, s):
        groups = window_groups(h)
        if isinstance(h, int) and h < 0:
            return list(enumerate(groups))
        return [(n, g) for n, g in enumerate(groups) if (g[1] == s - 2 if g[0] == "a" else g[1] == s)]

    qk_loaded, v_loaded, g_loaded = sem("qk_loaded"), sem("v_loaded"), sem("g_loaded")
    consts_set = sem("consts_set")
    qk_hi_ready, qk_lo_ready = sem("qk_hi_ready"), sem("qk_lo_ready")
    s_ready, s_taken, p_ready, a_ready = sem("s_ready"), sem("s_taken"), sem("p_ready"), sem("a_ready")
    tr_ready, tr_hi_ready, tr_taken = sem("tr_ready"), sem("tr_hi_ready"), sem("tr_taken")
    o_ready, o_taken = sem("o_ready"), sem("o_taken")
    o_ms_ready, o_rstd_ready, o_normed = sem("o_ms_ready"), sem("o_rstd_ready"), sem("o_normed")
    og_ready, og_stored = sem("og_ready"), [sem(f"og_stored{i}") for i in range(2)]
    inv_ready, ratio_ready, bias_step, iota_ready = sem("inv_ready"), sem("ratio_ready"), sem("bias_step"), sem("iota_ready")

    def windows(eng, window):
        window(0, 0)
        window(1, 1)
        with eng.Fori(1, H // 2 - 1) as pair:
            window(2 * pair, 0)
            window(2 * pair + 1, 1)
        window(H - 2, 0)
        window(H - 1, 1)
        window(H, 0)

    def has(h, what):
        if not isinstance(h, int):
            return True
        return {"last": h > 0, "own": h < H, "next": h < H - 1, "second": h < H - 2}[what]

    ctx = ExitStack()
    with ctx:
        s_ps = [ctx.enter_context(nc.psum_tensor(f"s_ps{i}", [P, S], F32)) for i in range(2)]
        tr_ps = [ctx.enter_context(nc.psum_tensor(f"tr_ps{i}", [P, 512], F32)) for i in range(2)]
        o_ps = [ctx.enter_context(nc.psum_tensor(f"o_ps{i}", [P, 2 * DV], F32)) for i in range(2)]
        block = ctx.enter_context(nc.Block())

        def lag(h, s, back):
            place = s - back
            if place >= 0:
                return has(h, "own"), h, place
            return has(h, "last"), h - 1, place + NT

        @block.sync
        def _(sp):
            def load_qk(h):
                after(sp, qk_hi_ready, 4 * h)
                after(sp, qk_lo_ready, 4 * h)
                for j, first in enumerate((Q_BLOCK0, K_BLOCK0)):
                    sp.dma_start(qk_raw[:, 2 * j:2 * j + 2, :], u_dram[bass.ds(2 * h + first, 2)].rearrange("b p s -> p b s")).then_inc(qk_loaded, 16)

            def load_v(h, transposed):
                after(sp, tr_ready, transposed)
                sp.dma_start(v_raw[:], u_dram[bass.ds(2 * h + V_BLOCK0, 2)].rearrange("b p s -> p b s")).then_inc(v_loaded, 16)

            load_qk(0)
            load_v(0, 0)
            load_qk(1)
            load_v(1, made(-1, PROLOGUE, 4))

            def window(h, par):
                if has(h, "last"):
                    after(sp, og_ready, 4 * (h - 1))
                    sp.dma_start(gate[:], u_dram[bass.ds(2 * (h - 1) + G_BLOCK0, 2)].rearrange("b p s -> p b s")).then_inc(g_loaded, 16)
                if has(h, "second"):
                    load_qk(h + 2)
                    groups = window_groups(h)
                    load_v(h + 2, made(h, groups, max(n for n, g in enumerate(groups) if g[0] == "v") + 1))
                if has(h, "last"):
                    for g in range(4):
                        sp.wait_ge(og_ready, 4 * (h - 1) + (g + 1))
                        row = (2 * (h - 1) + g // 2)
                        sp.dma_start(og_dram[bass.ds(row, 1), :, (g % 2) * 512:(g % 2 + 1) * 512].rearrange("o p s -> p (o s)"),
                                     og_out[g % 2][:]).then_inc(og_stored[g % 2], 16)

            windows(sp, window)
            for b in range(2):
                sp.wait_ge(og_stored[b], 16 * 2 * H)

        @block.gpsimd
        def _(pool):
            nc.gpsimd.memset(one_in_dv[:], 1.0 / DV).then_inc(consts_set, 1)
            nc.gpsimd.memset(eps[:], EPS).then_inc(consts_set, 1)
            pool.wait_ge(consts_set, 2)
            nc.gpsimd.iota(bias[1][:], pattern=[[-1, S]], base=S - P, channel_multiplier=1,
                           allow_small_or_imprecise_dtypes=True).then_inc(iota_ready, 1)
            pool.wait_ge(iota_ready, 1)
            nc.gpsimd.tensor_scalar(bias[1][:], bias[1][:], -1.0 / SCALE, None, ALU.mult).then_inc(iota_ready, 1)
            pool.wait_ge(iota_ready, 2)
            nc.gpsimd.affine_select(out=bias[1][:], in_=bias[1][:], compare_op=ALU.is_ge, fill=MASKED, base=S - P,
                                    pattern=[[-1, S]], channel_multiplier=1).then_inc(iota_ready, 1)

            def split_lo(h, par):
                for j in range(4):
                    pool.wait_ge(qk_hi_ready, 4 * h + (j + 1))
                    nc.gpsimd.tensor_tensor(qk_lo[par][:, j, :], qk_raw[:, j, :], qk_hi[par][:, j, :].bitcast(F32), ALU.subtract).then_inc(qk_lo_ready, 1)

            split_lo(0, 0)

            def window(h, par):
                if has(h, "next"):
                    split_lo(h + 1, 1 - par)
                if has(h, "last"):
                    prev = 1 - par
                    pool.wait_ge(o_taken, 8 * h)
                    nc.gpsimd.tensor_tensor(o_ssq[prev][:], o_ssq[prev][:], one_in_dv[:], ALU.mult).then_inc(o_ms_ready, 1)
                    pool.wait_ge(o_ms_ready, 2 * h - 1)
                    nc.gpsimd.tensor_tensor(o_ssq[prev][:], o_ssq[prev][:], eps[:], ALU.add).then_inc(o_ms_ready, 1)
                    pool.wait_ge(o_ms_ready, 2 * h)
                    after(pool, o_normed, h - 1)
                    nc.gpsimd.tensor_tensor(o_rstd[:], o_ssq[prev][:], t.minus_half[:], ALU.pow).then_inc(o_rstd_ready, 1)
                    pool.wait_ge(o_rstd_ready, h)
                    nc.gpsimd.tensor_tensor(o[prev][:], o[prev][:], o_rstd[:].rearrange("p (n o) -> p n o", o=1).broadcast_to((P, NT, DV)),
                                            ALU.mult).then_inc(o_normed, 1)

            windows(pool, window)

        @block.scalar
        def _(act):
            def split_qk(h, par, j):
                act.wait_ge(qk_loaded, 32 * (h + 1))
                after(act, s_ready, 16 * (h - 1))
                nc.scalar.activation(qk_hi[par][:, j, :], qk_raw[:, j, :], ACT.Copy).then_inc(qk_hi_ready, 1)

            def split_v(h, groups, place, g, par):
                act.wait_ge(tr_ready, made(h, groups, place) + 1)
                after(act, o_ready, 8 * h)
                nc.scalar.activation(v_hi[par][:, 2 * g:2 * g + 2, :], tr_ps[bank_of(h, place)][:].rearrange("p (i d) -> p i d", i=2),
                                     ACT.Copy).then_inc(tr_hi_ready, 1)

            for j in range(4):
                split_qk(0, 0, j)
            for n, (_, _, g) in groups_at(-1, 0):
                split_v(-1, PROLOGUE, n, g, 0)

            def window(h, par):
                steps = range(NT) if has(h, "own") else range(4)
                groups = window_groups(h)
                for s in steps:
                    for n, (kind, _, g) in groups_at(h, s):
                        if kind == "a":
                            there, ah, place = lag(h, s, 2)
                            i = ORDER[place]
                            cols = slice(4 * g * P, min(4 * g + 4, i + 1) * P)
                            act.wait_ge(tr_ready, made(h, groups, n) + 1)
                            after(act, o_ready, 8 * h + s - 3)
                            nc.scalar.activation(aT_hi[s % 2][:, cols], tr_ps[bank_of(h, n)][:, 0:cols.stop - cols.start], ACT.Copy).then_inc(tr_hi_ready, 1)
                    if has(h, "own"):
                        i = ORDER[s]
                        width = (i + 1) * P
                        for m in range(2):
                            act.wait_ge(s_taken, 16 * h + (2 * s + m + 1))
                            after(act, a_ready, 8 * h + s - 1)
                            nc.scalar.activation(e[s % 2][m][:, 0:width], e[s % 2][m][:, 0:width], ACT.Exp, scale=-1.0,
                                                 bias=row_min[s % 2][:, m:m + 1], accum_out=row_sum[s % 2][:, m:m + 1]).then_inc(p_ready, 1)
                    there, oh, place = lag(h, s, 4)
                    if there:
                        op = par if place == s - 4 else 1 - par
                        i = ORDER[place]
                        act.wait_ge(o_ready, 8 * oh + place + 1)
                        if place == 0:
                            after(act, og_ready, 4 * (oh - 1))
                        after(act, o_taken, 8 * oh + place)
                        nc.scalar.activation(junk[:], o_ps[place % 2][:, 0:DV], ACT.Square, scale=row_inv[op][:, i, 0:1],
                                             accum_out=o_ssq[op][:, i:i + 1])
                        nc.scalar.activation(o[op][:, i, :], o_ps[place % 2][:, 0:DV], ACT.Copy, scale=row_inv[op][:, i, 0:1]).then_inc(o_taken, 1)
                    for n, (kind, _, g) in groups_at(h, s):
                        if kind == "v":
                            split_v(h, groups, n, g, 1 - par)
                    if has(h, "next") and s < 4:
                        split_qk(h + 1, 1 - par, s)

            windows(act, window)

        @block.vector
        def _(dve):
            def split_v(h, groups, place, g, par):
                dve.wait_ge(tr_hi_ready, split(h, groups, place) + 1)
                view = tr_ps[bank_of(h, place)][:].rearrange("p (i d) -> p i d", i=2)
                nc.vector.tensor_tensor(v_lo[par][:, 2 * g:2 * g + 2, :], view, v_hi[par][:, 2 * g:2 * g + 2, :].bitcast(F32), ALU.subtract).then_inc(tr_taken, 1)

            awaited = [dve.alloc_register(f"awaited{i}") for i in range(2)]
            dve.wait_ge(iota_ready, 3)
            for n, (_, _, g) in groups_at(-1, 0):
                split_v(-1, PROLOGUE, n, g, 0)

            def combine(h, par, place):
                q = place % 2
                i = ORDER[place]
                width = (i + 1) * P
                dve.wait_ge(p_ready, 16 * h + (2 * place + 2))
                after(dve, o_taken, 8 * (h - 1))
                nc.vector.reciprocal(row_inv[par][:, i, :], row_sum[q][:]).then_inc(inv_ready, 1)
                dve.wait_ge(inv_ready, 8 * h + (place + 1))
                nc.vector.scalar_tensor_tensor(out=ratio[:], in0=row_sum[q][:, 0:1], scalar=t.neg_lam[:], in1=row_inv[par][:, i, 1:2],
                                               op0=ALU.mult, op1=ALU.mult).then_inc(ratio_ready, 1)
                dve.wait_ge(ratio_ready, 8 * h + (place + 1))
                nc.vector.scalar_tensor_tensor(out=a[q][:, 0:width], in0=e[q][1][:, 0:width], scalar=ratio[:], in1=e[q][0][:, 0:width],
                                               op0=ALU.mult, op1=ALU.add).then_inc(a_ready, 1)

            def window(h, par):
                steps = range(NT)
                groups = window_groups(h)
                if has(h, "own"):
                    nc.vector.tensor_scalar(bias[par][:], bias[1 - par][:], 0.5, None, ALU.mult).then_inc(bias_step, 1)
                    dve.wait_ge(bias_step, h + 1)
                for s in steps:
                    if has(h, "own"):
                        i = ORDER[s]
                        width = (i + 1) * P
                        for m in range(2):
                            after_apart(dve, [(s_ready, 16 * h + (2 * s + m + 1)), (a_ready, 8 * h + (s - 1))], awaited)
                            nc.vector.tensor_tensor_reduce(out=e[s % 2][m][:, 0:width], in0=s_ps[m][:, 0:width], in1=bias[par][:, S - width:S],
                                                           scale=-SCALE, scalar=3.0e38, op0=ALU.add, op1=ALU.min,
                                                           accum_out=row_min[s % 2][:, m:m + 1]).then_inc(s_taken, 1)
                    there, ch, place = lag(h, s, 1)
                    if there:
                        combine(ch, par if place == s - 1 else 1 - par, place)
                    for n, (kind, _, g) in groups_at(h, s):
                        if kind == "a":
                            there, ah, place = lag(h, s, 2)
                            i = ORDER[place]
                            cols = slice(4 * g * P, min(4 * g + 4, i + 1) * P)
                            dve.wait_ge(tr_hi_ready, split(h, groups, n) + 1)
                            nc.vector.tensor_tensor(aT_lo[s % 2][:, cols], tr_ps[bank_of(h, n)][:, 0:cols.stop - cols.start],
                                                    aT_hi[s % 2][:, cols].bitcast(F32), ALU.subtract).then_inc(tr_taken, 1)
                        elif kind == "v":
                            split_v(h, groups, n, g, 1 - par)
                        else:
                            dve.wait_ge(tr_ready, made(h, groups, n) + 1)
                            dve.wait_ge(g_loaded, 16 * h)
                            after(dve, og_stored[g % 2], 16 * (2 * (h - 1) + g // 2))
                            d, half = g // 2, g % 2
                            nc.vector.scalar_tensor_tensor(out=og_out[half][:], in0=tr_ps[bank_of(h, n)][:], scalar=t.subln_col[:, d:d + 1],
                                                           in1=gate[:, d, half * 512:(half + 1) * 512], op0=ALU.mult, op1=ALU.mult).then_inc(og_ready, 1)

            windows(dve, window)

        @block.tensor
        def _(pe):
            def transpose_v(h, groups, place, g):
                wait_bank(h, groups, place)
                bank = tr_ps[bank_of(h, place)]
                for i in range(2):
                    for d in range(2):
                        col = (2 * i + d) * P
                        last = nc.tensor.transpose(bank[:, col:col + P], v_raw[:, d, (2 * g + i) * P:(2 * g + i + 1) * P], t.ident[:])
                last.then_inc(tr_ready, 1)

            def wait_bank(h, groups, place):
                if place >= 1:
                    after_groups(h, groups[:place - 1])
                elif isinstance(h, int) and h <= -1:
                    return
                else:
                    after_previous(h)

            def after_groups(h, kinds):
                n_og = len([g for g in kinds if g[0] == "og"])
                after(pe, tr_taken, split(h, kinds, len(kinds)))
                if has(h, "last"):
                    after(pe, og_ready, (h - 1) * 4 + n_og)

            def after_previous(h):
                if isinstance(h, int) and h == 0:
                    after(pe, tr_taken, len(PROLOGUE) - 1)
                    return
                after(pe, tr_taken, split(h, [], 0) - (1 if isinstance(h, int) and h == 1 else 0))
                if not (isinstance(h, int) and h == 1):
                    after(pe, og_ready, (h - 1) * 4 - 1)

            pe.wait_ge(v_loaded, 16)
            for n, (_, _, g) in groups_at(-1, 0):
                transpose_v(-1, PROLOGUE, n, g)

            def scores(h, par, s):
                i = ORDER[s]
                width = (i + 1) * P
                for m in range(2):
                    after(pe, s_taken, 16 * h + (2 * s + m - 1))
                    for c0 in range(0, width, 512):
                        c1 = min(c0 + 512, width)
                        for j, (q, k) in enumerate(((qk_hi, qk_hi), (qk_hi, qk_lo), (qk_lo, qk_hi))):
                            last = nc.tensor.matmul(s_ps[m][:, c0:c1], q[par][:, m, i * P:(i + 1) * P], k[par][:, 2 + m, c0:c1],
                                                    start=(j == 0), stop=(j == 2))
                    last.then_inc(s_ready, 1)

            def products(h, par, place, window_h, window_s):
                q = place % 2
                i = ORDER[place]
                groups = window_groups(window_h)
                end = max(n for n, g in groups_at(window_h, window_s) if g[0] == "a") + 1
                pe.wait_ge(tr_taken, split(window_h, groups, end))
                after(pe, o_taken, 8 * h + (place - 1))
                for kt in range(i + 1):
                    rows = slice(kt * P, (kt + 1) * P)
                    for j, (x, v) in enumerate(((aT_hi, v_hi), (aT_hi, v_lo), (aT_lo, v_hi))):
                        last = nc.tensor.matmul(o_ps[q][:, 0:DV], x[q][:, rows], v[par][:, kt, :], start=(kt == 0 and j == 0), stop=(kt == i and j == 2))
                last.then_inc(o_ready, 1)

            def window(h, par):
                groups = window_groups(h)
                for s in range(NT):
                    for n, (kind, _, g) in groups_at(h, s):
                        if kind == "a":
                            there, ah, place = lag(h, s, 2)
                            i = ORDER[place]
                            pe.wait_ge(a_ready, 8 * ah + (place + 1))
                            wait_bank(h, groups, n)
                            for j in range(4 * g, min(4 * g + 4, i + 1)):
                                last = nc.tensor.transpose(tr_ps[bank_of(h, n)][:, (j - 4 * g) * P:(j - 4 * g + 1) * P],
                                                           a[place % 2][:, j * P:(j + 1) * P], t.ident[:])
                            last.then_inc(tr_ready, 1)
                    there, oh, place = lag(h, s, 3)
                    if there:
                        wh, ws = (h, s - 1) if s >= 1 else (h - 1, NT - 1)
                        products(oh, par if place == s - 3 else 1 - par, place, wh, ws)
                    for n, (kind, _, g) in groups_at(h, s):
                        if kind == "v":
                            pe.wait_ge(v_loaded, 16 * (h + 2))
                            transpose_v(h, groups, n, g)
                        elif kind == "og":
                            pe.wait_ge(o_normed, h)
                            wait_bank(h, groups, n)
                            d, half = g // 2, g % 2
                            for i in range(4):
                                last = nc.tensor.transpose(tr_ps[bank_of(h, n)][:, i * P:(i + 1) * P],
                                                           o[1 - par][:, 4 * half + i, d * P:(d + 1) * P], t.ident[:])
                            last.then_inc(tr_ready, 1)
                    if has(h, "own") and s < NT - 1:
                        scores(h, par, s + 1)
                    elif has(h, "next") and s == NT - 1:
                        pe.wait_ge(qk_lo_ready, 4 * (h + 2))
                        scores(h + 1, 1 - par, 0)

            pe.wait_ge(qk_lo_ready, 4)
            scores(0, 0, 0)
            windows(pe, window)


def output_projection(nc, sem, t, A, og_dram, out):
    put, at = region(nc, t.hi_at)
    og_raw = put("og_raw", [P, KT, S])
    z = put("z", [P, NT, D])
    og_hi = [put(f"og_hi{i}", [P, S], F32R) for i in range(2)]
    og_lo = [put(f"og_lo{i}", [P, S], F32R) for i in range(2)]
    w_raw = [put(f"wo_raw{i}", [P, NW]) for i in range(4)]
    w_hi = [put(f"wo_hi{i}", [P, NW], F32R) for i in range(2)]
    w_lo = [put(f"wo_lo{i}", [P, NW], F32R) for i in range(2)]
    gate_row = put("gate_row", [P, D])
    final_row = put("final_row", [P, D])
    gated = [put(f"gated{i}", [P, NW]) for i in range(4)]
    junk = put("z_squares", [P, D])
    z_ssq = put("z_ssq", [P, NT])
    z_rstd = put("z_rstd", [P, NT])
    assert at[0] <= nc.sbuf_usable_end

    wo_loaded = [sem(f"wo_loaded{i}") for i in range(4)]
    og_loaded = [sem(f"og_loaded{k}") for k in range(KT)]
    z_loaded, final_loaded = sem("z_loaded"), sem("final_loaded")
    og_hi_ready, og_lo_ready, wo_hi_ready, wo_lo_ready = sem("og_hi_ready"), sem("og_lo_ready"), sem("wo_hi_ready"), sem("wo_lo_ready")
    gate_ps_ready, gate_row_ready = sem("gate_ps_ready"), sem("gate_row_ready")
    step_done, y_ready, y_taken, z_added = sem("step_done"), sem("y_ready"), sem("y_taken"), sem("z_added")
    z_ssq_ready, z_ms_ready, z_rstd_ready, z_normed, stored = sem("z_ssq_ready"), sem("z_ms_ready"), sem("z_rstd_ready"), sem("z_normed"), sem("out_stored")

    ctx = ExitStack()
    with ctx:
        y_ps = [ctx.enter_context(nc.psum_tensor(f"y_ps{i}", [P, NW], F32)) for i in range(NT)]
        block = ctx.enter_context(nc.Block())

        @block.sync
        def _(sp):
            def load_w(n, k):
                after(sp, wo_lo_ready, KT * n + (k - 3))
                sp.dma_start(w_raw[k % 4][:], A["attn_w_out"][0][k * P:(k + 1) * P, bass.ds(n * NW, NW)]).then_inc(wo_loaded[k % 4], 16)

            for k in range(KT):
                load_w(0, k)
                sp.dma_start(og_raw[:, k, :], og_dram[k]).then_inc(og_loaded[k], 16)
            for m in range(NT):
                sp.dma_start(z[:, m, :], A["x"][0, m * P:(m + 1) * P, :]).then_inc(z_loaded, 16)
            sp.dma_start(final_row[:], A["final_g"].rearrange("(o n) -> o n", o=1).broadcast_to((P, D))).then_inc(final_loaded, 16)
            with sp.Fori(1, OUT_N) as n:
                for k in range(KT):
                    load_w(n, k)
            for m in range(NT):
                sp.wait_ge(z_normed, m + 1)
                sp.dma_start(out[0, m * P:(m + 1) * P, :], z[:, m, :]).then_inc(stored, 16)
            sp.wait_ge(stored, 16 * NT)

        @block.scalar
        def _(act):
            def split_hi(n, k):
                act.wait_ge(wo_loaded[k % 4], 64 * n + 16 * (k // 4 + 1))
                after(act, step_done, KT * n + (k - 1))
                nc.scalar.activation(w_hi[k % 2][:], w_raw[k % 4][:], ACT.Copy).then_inc(wo_hi_ready, 1)
                act.wait_ge(og_loaded[k], 16)
                nc.scalar.activation(og_hi[k % 2][:], og_raw[:, k, :], ACT.Copy).then_inc(og_hi_ready, 1)

            act.wait_ge(gate_ps_ready, 1)
            for n in range(OUT_N):
                nc.scalar.activation(gate_row[:, n * NW:(n + 1) * NW], y_ps[n][:], ACT.Copy).then_inc(gate_row_ready, 1)
            for k in range(KT):
                split_hi(0, k)
            with act.Fori(1, OUT_N) as n:
                for k in range(KT):
                    split_hi(n, k)
            for m in range(NT):
                act.wait_ge(z_added, NT * (OUT_N - 1) + m + 1)
                after(act, z_ssq_ready, m)
                nc.scalar.activation(junk[:], z[:, m, :], ACT.Square, accum_out=z_ssq[:, m:m + 1]).then_inc(z_ssq_ready, 1)

        @block.vector
        def _(dve):
            def split_lo(n, k):
                dve.wait_ge(wo_hi_ready, KT * n + (k + 1))
                nc.vector.tensor_tensor(w_lo[k % 2][:], w_raw[k % 4][:], w_hi[k % 2][:].bitcast(F32), ALU.subtract).then_inc(wo_lo_ready, 1)
                dve.wait_ge(og_hi_ready, KT * n + (k + 1))
                nc.vector.tensor_tensor(og_lo[k % 2][:], og_raw[:, k, :], og_hi[k % 2][:].bitcast(F32), ALU.subtract).then_inc(og_lo_ready, 1)

            def take(n):
                for m in range(NT):
                    if m < NT - 1:
                        dve.wait_ge(y_ready, (NT - 1) * n + (m + 1))
                    else:
                        dve.wait_ge(step_done, KT * (n + 1))
                    after(dve, z_added, NT * n + (m - 3))
                    nc.vector.tensor_tensor(gated[m % 4][:], y_ps[m][:], gate_row[:, bass.ds(n * NW, NW)], ALU.mult).then_inc(y_taken, 1)

            for k in range(KT):
                split_lo(0, k)
            dve.wait_ge(gate_row_ready, OUT_N)

            def chunk(n):
                split_lo(n, 0)
                split_lo(n, 1)
                take(n - 1)
                for k in range(2, KT):
                    split_lo(n, k)

            chunk(1)
            with dve.Fori(2, OUT_N) as n:
                chunk(n)
            take(OUT_N - 1)
            dve.wait_ge(final_loaded, 16)
            for m in range(NT):
                dve.wait_ge(z_rstd_ready, m + 1)
                nc.vector.scalar_tensor_tensor(out=z[:, m, :], in0=z[:, m, :], scalar=z_rstd[:, m:m + 1], in1=final_row[:],
                                               op0=ALU.mult, op1=ALU.mult).then_inc(z_normed, 1)

        @block.gpsimd
        def _(pool):
            def add(n, m):
                pool.wait_ge(y_taken, NT * n + (m + 1))
                part = z[:, m, bass.ds(n * NW, NW)]
                nc.gpsimd.tensor_tensor(part, part, gated[m % 4][:], ALU.add).then_inc(z_added, 1)

            pool.wait_ge(z_loaded, 16 * NT)
            with pool.Fori(0, OUT_N - 1) as n:
                for m in range(NT):
                    add(n, m)
            for m in range(NT):
                add(OUT_N - 1, m)
            for m in range(NT):
                pool.wait_ge(z_ssq_ready, m + 1)
                nc.gpsimd.tensor_scalar(z_ssq[:, m:m + 1], z_ssq[:, m:m + 1], 1.0 / D, EPS, ALU.mult, ALU.add).then_inc(z_ms_ready, 1)
                pool.wait_ge(z_ms_ready, m + 1)
                nc.gpsimd.tensor_tensor(z_rstd[:, m:m + 1], z_ssq[:, m:m + 1], t.minus_half[:, 0:1], ALU.pow).then_inc(z_rstd_ready, 1)

        @block.tensor
        def _(pe):
            for n in range(OUT_N):
                last = nc.tensor.matmul(y_ps[n][:], t.ones[:], t.gate_acc[:, n * NW:(n + 1) * NW], start=True, stop=True)
            last.then_inc(gate_ps_ready, 1)
            pe.wait_ge(gate_row_ready, OUT_N)

            def chunk(n):
                for k in range(KT):
                    pe.wait_ge(og_lo_ready, KT * n + (k + 1))
                    for m in range(NT):
                        if k == 0:
                            after(pe, y_taken, NT * n + (m + 1 - NT))
                        rows = slice(m * P, (m + 1) * P)
                        for j, (x, w) in enumerate(((og_hi, w_hi), (og_hi, w_lo), (og_lo, w_hi))):
                            last = nc.tensor.matmul(y_ps[m][:], x[k % 2][:, rows], w[k % 2][:], start=(k == 0 and j == 0),
                                                    stop=(k == KT - 1 and j == 2))
                        if k == KT - 1 and m < NT - 1:
                            last.then_inc(y_ready, 1)
                    last.then_inc(step_done, 1)

            chunk(0)
            with pe.Fori(1, OUT_N) as n:
                chunk(n)


class Shared:
    pass


def hybrid_diffattn_kernel(nc, A, out):
    u_dram = nc.dram_tensor("u_T", [64, P, S], F32, kind="Internal")
    og_dram = nc.dram_tensor("og_T", [KT, P, S], F32, kind="Internal")
    t = Shared()
    put, at = region(nc, SBUF_BASE)
    t.ident = put("ident", [P, P])
    t.ones = put("ones", [P, P])
    t.minus_half = put("minus_half", [P, NT])
    t.c_act = put("c_act", [P, KT])
    t.subln_col = put("subln_col", [P, 2])
    t.neg_lam = put("neg_lam", [P, 1])
    t.gate_acc = put("gate_acc", [P, D])
    t.hi_at = at[0]
    t.h_hi = put("h_hi", [P, KT, S], F32R)
    t.lo_at = at[0]
    t.h_lo = put("h_lo", [P, KT, S], F32R)
    t.free_at = at[0]
    t.xT = nc.alloc_sbuf_tensor_at("x_normed_T", [P, KT, S], F32, offset=t.hi_at)
    with ExitStack() as ctx:
        def sem(name):
            return ctx.enter_context(nc.semaphore(name))

        t.after_w = place_weights(nc, t)
        t.proj_ready, t.w_hi_ready, t.w_lo_ready = sem("proj_ready"), sem("w_hi_ready"), sem("w_lo_ready")
        with ExitStack() as banks:
            t.early_ps = [banks.enter_context(nc.psum_tensor(f"early_ps{i}", [P, S], F32)) for i in range(EARLY)]
            t.late_ps = banks.enter_context(nc.psum_tensor("late_ps", [P, S], F32))
            modulation_and_first_blocks(nc, sem, t, A)
            input_projection(nc, sem, t, A, u_dram)
        attention(nc, sem, t, u_dram, og_dram)
        output_projection(nc, sem, t, A, og_dram, out)


_INS = ["x", "c", "norm_g", "ada_w", "ada_b", "attn_w_in", "attn_w_out", "attn_lam_q1", "attn_lam_k1", "attn_lam_q2",
        "attn_lam_k2", "attn_subln_g", "final_g"]


def kernel(**inputs):
    import numpy as _np
    import concourse.bacc as _bacc
    from concourse import mybir as _mybir
    from concourse.bass_utils import run_bass_kernel_spmd as _run

    nc = _bacc.Bacc("TRN2", target_bir_lowering=False, num_devices=1)
    arrays, args = {}, {}
    for name in _INS:
        a = _np.ascontiguousarray(inputs[name])
        arrays[f"in_{name}_dram"] = a
        args[name] = nc.dram_tensor(f"in_{name}_dram", a.shape, _mybir.dt.from_np(a.dtype), kind="ExternalInput").ap()
    out = nc.dram_tensor("out_dram", (1, S, D), _mybir.dt.float32, kind="ExternalOutput").ap()
    hybrid_diffattn_kernel(nc, args, out)
    r = _run(nc, [arrays], core_ids=[0])
    return r.results[0]["out_dram"]
```

```python
from contextlib import ExitStack
import math

import concourse.bass as bass
from concourse import mybir

F32 = mybir.dt.float32
F32R = mybir.dt.float32r
ALU = mybir.AluOpType
ACT = mybir.ActivationFunctionType

P = 128
D = 2048
S = 1024
KT = D // P
NT = S // P
H = 8
DK = 128
DV = 256
EPS = 1e-6
SCALE = DK ** -0.5
LAM_INIT = 0.8 - 0.6 * math.exp(-0.3 * 0)
MASKED = -1.0e37
HALF = S // 2

CHUNKS = 32
GATE_CHUNK, V_CHUNK = 16, 24
ADA_PARTS = KT
QUARTERS = 4
PAIR = 2 * P
PAIRS = KT // 2
EARLY = 3
Q_BLOCK0, K_BLOCK0, G_BLOCK0, V_BLOCK0 = 0, 16, 32, 48

ORDER = [7, 4, 6, 5, 0, 3, 1, 2]
OUT_N = 4
NW = D // OUT_N

OG_AHEAD = 12

SBUF_BASE = 16512


def region(nc, start):
    at = [start]

    def put(name, shape, dtype=F32):
        t = nc.alloc_sbuf_tensor_at(name, shape, dtype, offset=at[0])
        size = 4
        for n in shape[1:]:
            size *= n
        at[0] += (size + 31) // 32 * 32
        return t

    return put, at


def after(eng, sem, count):
    if isinstance(count, int) and count <= 0:
        return
    eng.wait_ge(sem, count)


def after_apart(eng, waits, held):
    for (_, count), register in zip(waits, held):
        if not isinstance(count, int):
            eng.reg_mov(register, count)
    if not isinstance(waits[0][1], int):
        eng.wait_ge(waits[0][0], 1)
    for (sem, count), register in zip(waits, held):
        after(eng, sem, count if isinstance(count, int) else register)


def place_weights(nc, t):
    put, at = region(nc, t.free_at)
    t.w_raw = put("w_raw", [P, KT, 2 * P])
    t.w_hi, t.w_lo = [], []
    for i in range(2):
        t.w_hi.append(put(f"w_hi{i}", [P, KT, P], F32R))
        t.w_lo.append(put(f"w_lo{i}", [P, KT, P], F32R))
    return at[0]


def place_ahead(nc, sem, t):
    put, _ = region(nc, t.free_at)
    t.qk_raw = put("qk_raw", [P, 4, S])
    t.qk_hi0 = put("qk_hi0", [P, 4, S], F32R)
    t.qk_lo0 = put("qk_lo0", [P, 4, S], F32R)
    put, at = region(nc, t.after_w + 4 * 3 * S)
    t.v_raw = put("v_raw", [P, 2, S])
    t.after_v_raw = at[0]
    put, at = region(nc, t.hi_at)
    t.wo_raw = [put(f"wo_raw{i}", [P, NW]) for i in range(4)]
    t.after_wo = at[0]
    put, at = region(nc, t.free_at)
    t.og_raw = put("og_raw", [P, KT, S])
    t.after_og = at[0]
    t.qk_loaded, t.v_loaded, t.qk_hi_ready = sem("qk_loaded"), sem("v_loaded"), sem("qk_hi_ready")
    t.u_stored = [sem(f"u_stored{i}") for i in range(2)]
    t.og_stored = sem("og_stored")
    t.wo_loaded = [sem(f"wo_loaded{i}") for i in range(4)]
    t.og_loaded = [sem(f"og_loaded{k}") for k in range(KT)]


def modulation_and_first_blocks(nc, sem, t, A):
    w_raw, w_hi, w_lo = t.w_raw, t.w_hi, t.w_lo
    put, _ = region(nc, t.lo_at)
    xt = [put(f"x_tile{i}", [P, D]) for i in range(NT)]
    put, at = region(nc, t.free_at)
    ada = [put(f"ada_piece{i}", [P, ADA_PARTS // QUARTERS, 2, PAIR]) for i in range(QUARTERS - 1)]
    h = put("h", [P, 2, S])
    junk = nc.alloc_sbuf_tensor_at("squares", [P, D], F32, offset=at[0] - 4 * D)
    ada.append(put("ada_piece_last", [P, ADA_PARTS // QUARTERS, 2, PAIR]))
    put, at = region(nc, t.after_w)
    we_raw = [put(f"early_w_raw{j}", [P, EARLY * P]) for j in range(2)]
    we_hi = [put(f"early_w_hi{j}", [P, EARLY * P], F32R) for j in range(2)]
    we_lo = [put(f"early_w_lo{j}", [P, EARLY * P], F32R) for j in range(2)]
    acc = [put(f"ada_sum{i}", [P, 2, PAIR]) for i in range(2)]
    vec_rows = put("vector_rows", [70, P])
    c_col = put("c_col", [P, KT])
    c_exp = put("c_exp", [P, KT])
    vec_cols = put("vector_cols", [P, 70])
    x_ssq = put("x_ssq", [P, NT])
    x_rstd = put("x_rstd", [P, NT])
    lam_prod = put("lam_prod", [P, 2])
    lam_exp = put("lam_exp", [P, 2])
    mod_cols = put("mod_cols", [P, 2, KT])
    gain_cols = put("gain_cols", [P, KT])
    assert at[0] <= nc.sbuf_usable_end

    small_loaded, x_loaded = sem("small_loaded"), [sem(f"x_loaded{m}") for m in range(NT)]
    ada_loaded = [sem(f"ada_loaded{s}") for s in range(QUARTERS)]
    we_loaded, w_loaded = [sem(f"early_w_loaded{j}") for j in range(2)], sem("w_first_loaded")
    ones_set, ident_zero, ident_set = sem("ones_set"), sem("ident_zero"), sem("ident_set")
    c_step, c_exp_ready, c_ready = sem("c_step"), sem("c_exp_ready"), sem("c_ready")
    ssq_ready, ms_ready, rstd_ready, x_scaled = sem("ssq_ready"), sem("ms_ready"), sem("rstd_ready"), sem("x_scaled")
    xT_ready, xT_by_act, xT_by_dve = sem("xT_ready"), sem("xT_taken_by_act"), sem("xT_taken_by_dve")
    vec_ready, vec_taken, lam_prod_ready, lam_sum_ready = sem("vec_ready"), sem("vec_taken"), sem("lam_prod_ready"), sem("lam_sum_ready")
    lam_exp_ready = sem("lam_exp_ready")
    ada_summed, ada_multiplied, mod_ready, mod_added, gain_ready = sem("ada_summed"), sem("ada_multiplied"), sem("mod_ready"), sem("mod_added"), sem("gain_ready")
    h_ready, h_hi_ready, h_lo_ready = sem("h_ready"), sem("h_hi_ready"), sem("h_lo_ready")
    we_hi_ready, we_lo_ready, pair_done = sem("early_w_hi_ready"), sem("early_w_lo_ready"), sem("early_products")

    ROWS = ADA_PARTS // QUARTERS
    SUMS = (ROWS - 1) * QUARTERS

    def xT_ps(n):
        bank = t.early_ps[n % 6 // 2]
        return bank[:, n % 2 * 512:(n % 2 + 1) * 512]

    vec_ps = t.late_ps[:, 0:512]
    mod_ps = t.late_ps[:, 512:516].rearrange("p (m k) -> p m k", m=2)

    def pairs(body):
        for q in range(PAIRS + 1):
            body(q, q % 2)

    def is_pair(q):
        return q < PAIRS

    def has_last(q, back=1):
        return q >= back

    block = ExitStack()
    with block as ctx:
        block = ctx.enter_context(nc.Block())

        @block.sync
        def _(sp):
            sp.dma_start(c_col[:], A["c"][0].rearrange("(p t) -> p t", t=KT)).then_inc(small_loaded, 16)
            rows = A["ada_b"][0].rearrange("(j p) -> j p", p=P)
            sp.dma_start(vec_rows[0:48, :], rows).then_inc(small_loaded, 16)
            sp.dma_start(vec_rows[48:64, :], A["norm_g"][0].rearrange("(j p) -> j p", p=P)).then_inc(small_loaded, 16)
            sp.dma_start(vec_rows[64:66, :], A["attn_subln_g"][0].rearrange("(j p) -> j p", p=P)).then_inc(small_loaded, 16)
            for j, name in enumerate(("attn_lam_q1", "attn_lam_k1", "attn_lam_q2", "attn_lam_k2")):
                sp.dma_start(vec_rows[66 + j:67 + j, :], A[name]).then_inc(small_loaded, 16)
            for m in range(NT):
                sp.dma_start(xt[m][:], A["x"][0, m * P:(m + 1) * P, :]).then_inc(x_loaded[m], 16)
            ada_rows = A["ada_w"][0].rearrange("(p t) (m n) -> p t m n", t=ADA_PARTS, m=3)

            def load_we(q, j):
                after(sp, we_hi_ready, 2 * (q - 1) + j + 1 if has_last(q) else 0)
                after(sp, we_lo_ready, 2 * (q - 1) + j + 1 if has_last(q) else 0)
                sp.dma_start(we_raw[j][:], A["attn_w_in"][0][q * PAIR + j * P:q * PAIR + (j + 1) * P, 0:EARLY * P]).then_inc(we_loaded[j], 16)

            def body(q, par):
                for s in range(QUARTERS):
                    if s % 2 == 0 and has_last(q):
                        load_we(q - 1, s // 2)
                    if is_pair(q):
                        if has_last(q):
                            sp.wait_ge(ada_summed, SUMS * (q - 1) + (ROWS - 1) * (s + 1))
                            sp.wait_ge(ada_multiplied, QUARTERS * (q - 1) + s + 1)
                        for m in range(2):
                            sp.dma_start(ada[s][:, :, m, :], ada_rows[:, s * ROWS:(s + 1) * ROWS, m, q * PAIR:(q + 1) * PAIR]).then_inc(ada_loaded[s], 16)

            pairs(body)
            sp.wait_ge(ada_summed, SUMS * (PAIRS - 1) + (ROWS - 1) * 2)
            sp.wait_ge(ada_multiplied, QUARTERS * (PAIRS - 1) + 2)
            sp.dma_start(w_raw[:, :, P:2 * P], A["attn_w_in"][0][:, EARLY * P:(EARLY + 1) * P].rearrange("(k p) n -> p k n", p=P)).then_inc(w_loaded, 16)

        @block.gpsimd
        def _(pool):
            nc.gpsimd.memset(t.ident[:], 0.0).then_inc(ident_zero, 1)
            pool.wait_ge(ident_zero, 1)
            nc.gpsimd.affine_select(out=t.ident[:], in_=t.ident[:], compare_op=ALU.not_equal, fill=1.0, base=0,
                                    pattern=[[-1, P]], channel_multiplier=1).then_inc(ident_set, 1)
            nc.gpsimd.memset(t.ones[:], 1.0).then_inc(ones_set, 1)
            nc.gpsimd.memset(t.minus_half[:], -0.5).then_inc(ones_set, 1)
            pool.wait_ge(ones_set, 2)
            for m in range(NT):
                pool.wait_ge(ssq_ready, m + 1)
                nc.gpsimd.tensor_scalar(x_ssq[:, m:m + 1], x_ssq[:, m:m + 1], 1.0 / D, EPS, ALU.mult, ALU.add).then_inc(ms_ready, 1)
                pool.wait_ge(ms_ready, m + 1)
                nc.gpsimd.tensor_tensor(x_rstd[:, m:m + 1], x_ssq[:, m:m + 1], t.minus_half[:, 0:1], ALU.pow).then_inc(rstd_ready, 1)

            def body(q, par):
                if not has_last(q):
                    return
                for j in range(2):
                    pool.wait_ge(we_hi_ready, 2 * (q - 1) + j + 1)
                    nc.gpsimd.tensor_tensor(we_lo[j][:], we_raw[j][:], we_hi[j][:].bitcast(F32), ALU.subtract).then_inc(we_lo_ready, 1)

            pairs(body)

        @block.scalar
        def _(act):
            act.wait_ge(small_loaded, 128)
            nc.scalar.activation(c_exp[:], c_col[:], ACT.Exp, scale=-1.0).then_inc(c_exp_ready, 1)

            def square(m):
                act.wait_ge(x_loaded[m], 16)
                after(act, ssq_ready, m)
                nc.scalar.activation(junk[:], xt[m][:], ACT.Square, accum_out=x_ssq[:, m:m + 1]).then_inc(ssq_ready, 1)

            def take(m):
                for g in range(2):
                    n = 4 * m + g
                    act.wait_ge(xT_ready, n + 1)
                    nc.scalar.activation(t.xT[:, 4 * g:4 * g + 4, m * P:(m + 1) * P], xT_ps(n).rearrange("p (k s) -> p k s", k=4),
                                         ACT.Copy).then_inc(xT_by_act, 1)

            for m in range(NT):
                square(m)
                if m == 0:
                    act.wait_ge(lam_sum_ready, 1)
                    nc.scalar.activation(lam_exp[:], vec_ps[:, 96:98], ACT.Exp).then_inc(lam_exp_ready, 1)
                if m > 0:
                    take(m - 1)
            take(NT - 1)

            def body(q, par):
                if not has_last(q):
                    return
                if q == 1:
                    act.wait_ge(xT_by_act, 2 * NT)
                    act.wait_ge(xT_by_dve, 2 * NT)
                    act.wait_ge(ssq_ready, NT)

                def split(j):
                    act.wait_ge(we_loaded[j], 16 * q)
                    if has_last(q, 2):
                        act.wait_ge(pair_done, 2 * (q - 2) + j + 1)
                    nc.scalar.activation(we_hi[j][:], we_raw[j][:], ACT.Copy).then_inc(we_hi_ready, 1)

                split(0)
                for j in range(2):
                    if j == 0:
                        act.wait_ge(gain_ready, q)
                    if has_last(q, 2):
                        act.wait_ge(h_lo_ready, 2 * (q - 2) + j + 1)
                    k = 2 * (q - 1) + j
                    nc.scalar.activation(h[:, j, :], t.xT[:, k, :], ACT.Identity,
                                         bias=mod_cols[:, 0, k:k + 1], scale=gain_cols[:, k:k + 1]).then_inc(h_ready, 1)
                    act.wait_ge(h_ready, k + 1)
                    nc.scalar.activation(t.h_hi[:, k, :], h[:, j, :], ACT.Copy).then_inc(h_hi_ready, 1)
                split(1)

            pairs(body)
            act.wait_ge(w_loaded, 16)
            act.wait_ge(ada_summed, SUMS * PAIRS)
            act.wait_ge(ada_multiplied, QUARTERS * PAIRS)
            nc.scalar.activation(w_hi[1][:], w_raw[:, :, P:2 * P], ACT.Copy).then_inc(t.w_hi_ready, 1)

        @block.vector
        def _(dve):
            dve.wait_ge(c_exp_ready, 1)
            nc.vector.tensor_scalar_add(c_exp[:], c_exp[:], 1.0).then_inc(c_step, 1)
            dve.wait_ge(c_step, 1)
            nc.vector.reciprocal(c_exp[:], c_exp[:]).then_inc(c_step, 1)
            dve.wait_ge(c_step, 2)
            nc.vector.tensor_tensor(t.c_act[:], c_col[:], c_exp[:], ALU.mult).then_inc(c_ready, 1)
            dve.wait_ge(vec_ready, 1)
            nc.vector.tensor_copy(vec_cols[:], vec_ps[:, 0:70]).then_inc(vec_taken, 1)
            dve.wait_ge(vec_taken, 1)
            nc.vector.tensor_tensor(lam_prod[:], vec_cols[:, 66:70:2], vec_cols[:, 67:70:2], ALU.mult).then_inc(lam_prod_ready, 1)
            nc.vector.tensor_scalar(t.subln_col[:], vec_cols[:, 64:66], 1.0 - LAM_INIT, None, ALU.mult)

            def scale(m):
                dve.wait_ge(rstd_ready, m + 1)
                nc.vector.tensor_scalar(xt[m][:], xt[m][:], x_rstd[:, m:m + 1], None, ALU.mult).then_inc(x_scaled, 1)

            def take(m):
                for g in range(2, 4):
                    n = 4 * m + g
                    dve.wait_ge(xT_ready, n + 1)
                    nc.vector.tensor_copy(t.xT[:, 4 * g:4 * g + 4, m * P:(m + 1) * P],
                                          xT_ps(n).rearrange("p (k s) -> p k s", k=4)).then_inc(xT_by_dve, 1)

            def piece(q, par, s):
                dve.wait_ge(ada_loaded[s], 32 * (q + 1))
                for r in range(ROWS - 1):
                    n = (ROWS - 1) * s + r
                    c = t.c_act[:, s * ROWS + r:s * ROWS + r + 1]
                    if n == 0:
                        if has_last(q, 2):
                            dve.wait_ge(mod_ready, q - 1)
                        nc.vector.tensor_scalar(acc[par][:], ada[s][:, r], c, None, ALU.mult).then_inc(ada_summed, 1)
                    else:
                        dve.wait_ge(ada_summed, SUMS * q + n)
                        nc.vector.scalar_tensor_tensor(out=acc[par][:], in0=ada[s][:, r], scalar=c, in1=acc[par][:],
                                                       op0=ALU.mult, op1=ALU.add).then_inc(ada_summed, 1)

            for m in range(NT):
                scale(m)
                if m > 0:
                    take(m - 1)
            dve.wait_ge(c_ready, 1)
            piece(0, 0, 0)
            take(NT - 1)
            dve.wait_ge(lam_exp_ready, 1)
            nc.vector.scalar_tensor_tensor(out=t.neg_lam[:], in0=lam_exp[:, 1:2], scalar=-LAM_INIT, in1=lam_exp[:, 0:1],
                                           op0=ALU.add, op1=ALU.subtract)

            def columns(q):
                two = slice(2 * (q - 1), 2 * q)
                biases = vec_cols[:, 0:2 * KT].rearrange("p (m k) -> p m k", m=2)
                dve.wait_ge(mod_ready, q)
                nc.vector.tensor_tensor(mod_cols[:, :, two], mod_ps, biases[:, :, two], ALU.add).then_inc(mod_added, 1)
                dve.wait_ge(mod_added, q)
                nc.vector.scalar_tensor_tensor(out=gain_cols[:, two], in0=mod_cols[:, 1, two], scalar=1.0,
                                               in1=vec_cols[:, 48:64][:, two], op0=ALU.add, op1=ALU.mult).then_inc(gain_ready, 1)

            def h_lo(q, j):
                k = 2 * (q - 1) + j
                dve.wait_ge(h_hi_ready, k + 1)
                nc.vector.tensor_tensor(t.h_lo[:, k, :], h[:, j, :],
                                        t.h_hi[:, k, :].bitcast(F32), ALU.subtract).then_inc(h_lo_ready, 1)

            def body(q, par):
                if not has_last(q):
                    for s in range(1, QUARTERS):
                        piece(q, par, s)
                    dve.wait_ge(xT_ready, 4 * NT)
                    return
                if is_pair(q):
                    piece(q, par, 0)
                columns(q)
                if is_pair(q):
                    piece(q, par, 1)
                h_lo(q, 0)
                if is_pair(q):
                    piece(q, par, 2)
                h_lo(q, 1)
                if is_pair(q):
                    piece(q, par, 3)

            pairs(body)
            dve.wait_ge(t.w_hi_ready, 1)
            nc.vector.tensor_tensor(w_lo[1][:], w_raw[:, :, P:2 * P], w_hi[1][:].bitcast(F32), ALU.subtract).then_inc(t.w_lo_ready, 1)

        @block.tensor
        def _(pe):
            pe.wait_ge(ident_set, 1)
            pe.wait_ge(ones_set, 2)
            pe.wait_ge(small_loaded, 128)
            nc.tensor.transpose(vec_ps[:, 0:70], vec_rows[:], t.ident[0:70, 0:70]).then_inc(vec_ready, 1)
            pe.wait_ge(lam_prod_ready, 1)
            nc.tensor.matmul(vec_ps[:, 96:98], t.ones[:], lam_prod[:], start=True, stop=True).then_inc(lam_sum_ready, 1)
            for m in range(NT):
                pe.wait_ge(x_scaled, m + 1)
                for g in range(4):
                    after(pe, xT_by_dve if g < 2 else xT_by_act, 2 * (m - 2) + g + 1 if g < 2 else 2 * (m - 1) + g - 1)
                    for j in range(4):
                        k = 4 * g + j
                        last = nc.tensor.transpose(xT_ps(4 * m + g)[:, j * P:(j + 1) * P], xt[m][:, k * P:(k + 1) * P], t.ident[:])
                    last.then_inc(xT_ready, 1)

            def multiply(q, s):
                if s == 0:
                    if has_last(q):
                        pe.wait_ge(mod_added, q)
                    else:
                        pe.wait_ge(c_ready, 1)
                pe.wait_ge(ada_loaded[s], 32 * (q + 1))
                row = ROWS - 1
                for m in range(2):
                    for j in range(2):
                        last = nc.tensor.matmul(mod_ps[:, m, j:j + 1], ada[s][:, row, m, j * P:(j + 1) * P],
                                                t.c_act[:, s * ROWS + row:s * ROWS + row + 1], start=(s == 0 and m == 0 and j == 0), stop=False)
                last.then_inc(ada_multiplied, 1)

            def add_partitions(q, par):
                pe.wait_ge(ada_summed, SUMS * (q + 1))
                for m in range(2):
                    for j in range(2):
                        last = nc.tensor.matmul(mod_ps[:, m, j:j + 1], acc[par][:, m, j * P:(j + 1) * P], t.ones[:, 0:1], start=False,
                                                stop=(m == 1 and j == 1))
                last.then_inc(mod_ready, 1)

            def products(q, j):
                k = 2 * q + j
                first = k == 0
                if first:
                    pe.wait_ge(xT_by_act, 2 * NT)
                    pe.wait_ge(xT_by_dve, 2 * NT)
                pe.wait_ge(h_lo_ready, k + 1)
                pe.wait_ge(we_lo_ready, k + 1)
                last_k = k == KT - 1
                for b in range(EARLY):
                    for i, (w, h) in enumerate(((we_hi, t.h_hi), (we_hi, t.h_lo), (we_lo, t.h_hi))):
                        for half in range(2):
                            cols = slice(half * HALF, (half + 1) * HALF)
                            last = nc.tensor.matmul(t.early_ps[b][:, cols], w[j][:, b * P:(b + 1) * P],
                                                    h[:, k, cols], start=(first and i == 0), stop=(last_k and i == 2))
                    if last_k:
                        last.then_inc(t.proj_ready, 1)
                if not last_k:
                    last.then_inc(pair_done, 1)

            def body(q, par):
                if has_last(q, 2):
                    products(q - 2, 1)
                if is_pair(q):
                    multiply(q, 0)
                    multiply(q, 1)
                if has_last(q):
                    products(q - 1, 0)
                if is_pair(q):
                    multiply(q, 2)
                    multiply(q, 3)
                    add_partitions(q, par)
                else:
                    products(q - 1, 1)

            pairs(body)


def input_projection(nc, sem, t, A, u_dram):
    w_raw, w_hi, w_lo = t.w_raw, t.w_hi, t.w_lo
    put, at = region(nc, t.after_w)
    u_out = [put(f"u_out{i}", [P, S]) for i in range(2)]
    sig = put("sigmoid", [P, S])
    ada_gate = put("ada_gate_rows", [P, D])
    assert at[0] <= nc.sbuf_usable_end
    u_ps = [t.early_ps[0], t.late_ps]

    w_loaded, w_hi_ready, w_lo_ready = sem("w_loaded"), t.w_hi_ready, t.w_lo_ready
    proj_ready, proj_taken, u_free = t.proj_ready, sem("proj_taken"), t.u_stored
    gate_exp_ready, silu_step, silu_ready = sem("gate_exp_ready"), sem("silu_step"), sem("silu_ready")
    acc_zero, acc_row_loaded, ada_gate_loaded, gate_summed = sem("gate_acc_zero"), sem("gate_bias_loaded"), sem("ada_gate_loaded"), sem("gate_summed")
    C0 = 2
    C_ROWS = C0 + ADA_PARTS // 2

    ctx = ExitStack()
    with ctx:
        block = ctx.enter_context(nc.Block())

        @block.sync
        def _(sp):
            def load(c, shift=0):
                sp.wait_ge(w_hi_ready, 2 * c - EARLY)
                sp.wait_ge(w_lo_ready, 2 * c - EARLY)
                sp.dma_start(w_raw[:], A["attn_w_in"][0][:, bass.ds(c * 2 * P + shift * 2 * P, 2 * P)].rearrange("(k p) n -> p k n", p=P)).then_inc(w_loaded, 16)

            def load_gate_rows(c, b):
                r = 2 * (c - C0) + b
                after(sp, gate_summed, r)
                rows = A["ada_w"][0].rearrange("(p t) n -> p t n", t=ADA_PARTS)
                sp.dma_start(ada_gate[:], rows[:, bass.ds(r, 1), 2 * D:3 * D].rearrange("p o n -> p (o n)")).then_inc(ada_gate_loaded, 16)

            def store(c, b, gate=False):
                if gate:
                    sp.wait_ge(silu_ready, 2 * c + b - 2 * GATE_CHUNK + 1)
                else:
                    sp.wait_ge(proj_taken, 2 * c + b + 1)
                sp.dma_start(u_dram[bass.ds(2 * c + b, 1)].rearrange("o p s -> p (o s)"), u_out[b][:]).then_inc(u_free[b], 16)

            def chunk(c, gate=False, rows=False, more=True, shift=0):
                if rows:
                    load_gate_rows(c, 0)
                if more:
                    load(c + 1, shift)
                store(c, 0, gate)
                if rows:
                    load_gate_rows(c, 1)
                store(c, 1, gate)

            load(C0)
            for n in range(EARLY):
                store(n // 2, n % 2)
            sp.wait_ge(acc_zero, 1)
            sp.dma_start(t.gate_acc[0:1, :], A["ada_b"][:, 2 * D:3 * D]).then_inc(acc_row_loaded, 16)
            store(1, 1)
            chunk(C0, rows=True)
            with sp.Fori(C0 + 1, C_ROWS) as c:
                chunk(c, rows=True)
            with sp.Fori(C_ROWS, GATE_CHUNK - 1) as c:
                chunk(c)
            to_gate, to_v = V_CHUNK - GATE_CHUNK, GATE_CHUNK - V_CHUNK
            chunk(GATE_CHUNK - 1, shift=to_gate)
            with sp.Fori(GATE_CHUNK, V_CHUNK - 1) as c:
                chunk(c, gate=True, shift=to_gate)
            chunk(V_CHUNK - 1, gate=True, shift=to_v)
            with sp.Fori(V_CHUNK, CHUNKS - 1) as c:
                chunk(c, shift=to_v)
            sp.wait_ge(w_hi_ready, 2 * CHUNKS - EARLY)
            sp.wait_ge(w_lo_ready, 2 * CHUNKS - EARLY)
            sp.wait_ge(gate_summed, ADA_PARTS)
            for b in range(2):
                sp.wait_ge(u_free[b], 16 * (V_BLOCK0 // 2 + 1))
            load_head_qk(nc, sp, t, u_dram, 0)
            load_head_v(nc, sp, t, u_dram, 0)
            chunk(CHUNKS - 1, more=False)

        @block.scalar
        def _(act):
            def split_hi(c, b):
                act.wait_ge(w_loaded, 16 * (c - C0 + 1))
                act.wait_ge(proj_ready, 2 * c + b - 1)
                nc.scalar.activation(w_hi[b][:], w_raw[:, :, b * P:(b + 1) * P], ACT.Copy).then_inc(w_hi_ready, 1)

            def take(c, b, gate=False, banks=None):
                act.wait_ge(proj_ready, 2 * c + b + 1)
                after(act, u_free[b], 16 * c)
                if gate:
                    after(act, silu_ready, 2 * c + b - 2 * GATE_CHUNK)
                    nc.scalar.activation(sig[:], u_ps[b][:], ACT.Exp, scale=-1.0).then_inc(gate_exp_ready, 1)
                nc.scalar.activation(u_out[b][:], (banks or u_ps[b])[:], ACT.Copy).then_inc(proj_taken, 1)

            def chunk(c, gate=False, more=True):
                split_hi(c, 1)
                take(c, 0, gate)
                if more:
                    split_hi(c + 1, 0)
                else:
                    for j in range(4):
                        act.wait_ge(t.qk_loaded, 32)
                        act.wait_ge(proj_ready, 2 * c + 1)
                        nc.scalar.activation(t.qk_hi0[:, j, :], t.qk_raw[:, j, :], ACT.Copy).then_inc(t.qk_hi_ready, 1)
                take(c, 1, gate)

            for n in range(EARLY):
                take(n // 2, n % 2, banks=t.early_ps[n])
            split_hi(C0, 0)
            take(1, 1)
            with act.Fori(C0, GATE_CHUNK) as c:
                chunk(c)
            chunk(GATE_CHUNK, gate=True)
            with act.Fori(GATE_CHUNK + 1, V_CHUNK) as c:
                chunk(c, gate=True)
            with act.Fori(V_CHUNK, CHUNKS - 1) as c:
                chunk(c)
            chunk(CHUNKS - 1, more=False)

        @block.vector
        def _(dve):
            def split_lo(c, b):
                dve.wait_ge(w_hi_ready, 2 * c + b - EARLY + 1)
                nc.vector.tensor_tensor(w_lo[b][:], w_raw[:, :, b * P:(b + 1) * P], w_hi[b][:].bitcast(F32), ALU.subtract).then_inc(w_lo_ready, 1)

            def sum_gate(c, b):
                r = 2 * (c - C0) + b
                dve.wait_ge(ada_gate_loaded, 16 * (r + 1))
                after(dve, gate_summed, r)
                nc.vector.scalar_tensor_tensor(out=t.gate_acc[:], in0=ada_gate[:], scalar=t.c_act[:, bass.ds(r, 1)], in1=t.gate_acc[:],
                                               op0=ALU.mult, op1=ALU.add).then_inc(gate_summed, 1)

            def silu(c, b):
                n = 2 * c + b - 2 * GATE_CHUNK
                dve.wait_ge(gate_exp_ready, n + 1)
                nc.vector.tensor_scalar_add(sig[:], sig[:], 1.0).then_inc(silu_step, 1)
                dve.wait_ge(silu_step, 2 * n + 1)
                nc.vector.reciprocal(sig[:], sig[:]).then_inc(silu_step, 1)
                dve.wait_ge(silu_step, 2 * n + 2)
                dve.wait_ge(proj_taken, 2 * c + b + 1)
                nc.vector.tensor_tensor(u_out[b][:], u_out[b][:], sig[:], ALU.mult).then_inc(silu_ready, 1)

            def chunk(c, rows=False, gate=False, more=True):
                split_lo(c, 1)
                if rows:
                    sum_gate(c, 0)
                if gate:
                    silu(c, 0)
                if more:
                    split_lo(c + 1, 0)
                if rows:
                    sum_gate(c, 1)
                if gate:
                    silu(c, 1)

            nc.vector.memset(t.gate_acc[:], 0.0).then_inc(acc_zero, 1)
            split_lo(C0, 0)
            dve.wait_ge(acc_row_loaded, 16)
            chunk(C0, rows=True)
            with dve.Fori(C0 + 1, C_ROWS) as c:
                chunk(c, rows=True)
            with dve.Fori(C_ROWS, GATE_CHUNK) as c:
                chunk(c)
            with dve.Fori(GATE_CHUNK, V_CHUNK) as c:
                chunk(c, gate=True)
            with dve.Fori(V_CHUNK, CHUNKS - 1) as c:
                chunk(c)
            chunk(CHUNKS - 1, more=False)

        @block.tensor
        def _(pe):
            def product(c, b):
                pe.wait_ge(w_lo_ready, 2 * c + b - EARLY + 1)
                if not isinstance(c, int):
                    pe.wait_ge(proj_taken, 2 * c + b - 1)
                for k in range(KT):
                    for j, (w, h) in enumerate(((w_hi, t.h_hi), (w_hi, t.h_lo), (w_lo, t.h_hi))):
                        for half in range(2):
                            cols = slice(half * HALF, (half + 1) * HALF)
                            last = nc.tensor.matmul(u_ps[b][:, cols], w[b][:, k, :], h[:, k, cols],
                                                    start=(k == 0 and j == 0), stop=(k == KT - 1 and j == 2))
                last.then_inc(proj_ready, 1)

            product(1, 1)
            with pe.Fori(C0, CHUNKS) as c:
                product(c, 0)
                product(c, 1)


def load_head_qk(nc, sp, t, u_dram, h):
    for j, first in enumerate((Q_BLOCK0, K_BLOCK0)):
        sp.dma_start(t.qk_raw[:, 2 * j:2 * j + 2, :], u_dram[bass.ds(2 * h + first, 2)].rearrange("b p s -> p b s")).then_inc(t.qk_loaded, 16)


def load_head_v(nc, sp, t, u_dram, h):
    sp.dma_start(t.v_raw[:], u_dram[bass.ds(2 * h + V_BLOCK0, 2)].rearrange("b p s -> p b s")).then_inc(t.v_loaded, 16)


def load_out_w(sp, t, A, n, k):
    sp.dma_start(t.wo_raw[k % 4][:], A["attn_w_out"][0][k * P:(k + 1) * P, bass.ds(n * NW, NW)]).then_inc(t.wo_loaded[k % 4], 16)


def load_og(sp, t, og_dram, k):
    for half in range(2):
        sp.dma_start(t.og_raw[:, k, half * HALF:(half + 1) * HALF], og_dram[half][k]).then_inc(t.og_loaded[k], 16)


def attention(nc, sem, t, A, u_dram, og_dram):
    qk_raw, v_raw = t.qk_raw, t.v_raw
    put, at = region(nc, t.hi_at)
    v_hi = [put("v_hi0", [P, NT, DV], F32R)]
    v_lo = [put("v_lo0", [P, NT, DV], F32R)]
    gate = put("gate_T", [P, 2, S])
    qk_hi = [t.qk_hi0, put("qk_hi1", [P, 4, S], F32R)]
    qk_lo = [t.qk_lo0, put("qk_lo1", [P, 4, S], F32R)]
    v_hi.append(put("v_hi1", [P, NT, DV], F32R))
    v_lo.append(put("v_lo1", [P, NT, DV], F32R))
    e = [[put(f"e{i}{m}", [P, S]) for m in range(2)] for i in range(2)]
    a = [put(f"a{i}", [P, S]) for i in range(2)]
    aT_hi = [put(f"aT_hi{i}", [P, S], F32R) for i in range(2)]
    aT_lo = [put(f"aT_lo{i}", [P, S], F32R) for i in range(2)]
    o = [put(f"o{i}", [P, NT, DV]) for i in range(2)]
    assert at[0] <= t.free_at
    put, at = region(nc, t.after_w)
    bias = [put(f"alibi{i}", [P, S]) for i in range(2)]
    og_out = put("og_out", [P, 2, HALF])
    put, at = region(nc, t.after_v_raw)
    junk = put("o_squares", [P, DV])
    row_min = [put(f"row_min{i}", [P, 2]) for i in range(2)]
    row_sum = [put(f"row_sum{i}", [P, 2]) for i in range(2)]
    row_inv = [put(f"row_inv{i}", [P, NT, 2]) for i in range(2)]
    ratio = put("ratio", [P, 1])
    o_ssq = [put(f"o_ssq{i}", [P, NT]) for i in range(2)]
    o_rstd = put("o_rstd", [P, NT])
    one_in_dv = put("one_in_dv", [P, NT])
    eps = put("eps", [P, NT])
    assert at[0] <= nc.sbuf_usable_end

    V_STEPS = {2: (0,), 3: (1,), 4: (2,), 5: (3,)}
    OG_STEPS = {1: (0,), 2: (1,), 6: (2,), 7: (3,)}

    OG_STEPS_AT_END = {0: (0,), 1: (1,), 4: (2, 3)}

    def groups_of(s, first=False, has_next=True, has_tiles=True):
        found = []
        tile = s - 2
        if tile >= 0 and has_tiles or tile < 0 and not first:
            i = ORDER[tile % NT]
            found += [("a", tile, g) for g in range(i // 4 + 1)]
        if has_next:
            found += [("v", s, g) for g in V_STEPS.get(s, ())]
        if not first:
            found += [("og", s, g) for g in (OG_STEPS if has_tiles else OG_STEPS_AT_END).get(s, ())]
        return found

    def listed(**kinds):
        return [g for s in range(NT) for g in groups_of(s, **kinds)]

    PROLOGUE = [("v", -1, g) for g in range(4)]
    FIRST, STEADY = listed(first=True), listed()
    LAST = listed(has_next=False)

    def split_ones(groups):
        return [g for g in groups if g[0] != "og"]

    def made(h, groups, place):
        if isinstance(h, int) and h < 0:
            return place
        if isinstance(h, int) and h == 0:
            return len(PROLOGUE) + place
        short = len(STEADY) - len(LAST) if isinstance(h, int) and h == H else 0
        return (h - 1) * len(STEADY) + (len(PROLOGUE) + len(FIRST) + place - short)

    def split(h, groups, place):
        here = len(split_ones(groups[:place]))
        if isinstance(h, int) and h < 0:
            return here
        if isinstance(h, int) and h == 0:
            return len(PROLOGUE) + here
        short = len(STEADY) - len(LAST) if isinstance(h, int) and h == H else 0
        return (h - 1) * len(split_ones(STEADY)) + (len(PROLOGUE) + len(split_ones(FIRST)) + here - short)

    def bank_of(h, place):
        if isinstance(h, int) and h < 0:
            return place % 2
        if isinstance(h, int) and h == 0:
            return (len(PROLOGUE) + place) % 2
        return (len(PROLOGUE) + len(FIRST) + place) % 2

    assert len(STEADY) % 2 == 0

    def window_groups(h):
        if isinstance(h, int):
            if h < 0:
                return PROLOGUE
            if h == 0:
                return FIRST
            if h == H - 1:
                return LAST
            if h == H:
                return [g for s in range(NT) for g in groups_of(s, has_next=False, has_tiles=False)]
        return STEADY

    def groups_at(h, s):
        groups = window_groups(h)
        if isinstance(h, int) and h < 0:
            return list(enumerate(groups))
        return [(n, g) for n, g in enumerate(groups) if (g[1] == s - 2 if g[0] == "a" else g[1] == s)]

    qk_loaded, v_loaded, g_loaded = t.qk_loaded, t.v_loaded, sem("g_loaded")
    consts_set = sem("consts_set")
    qk_hi_ready, qk_lo_ready = t.qk_hi_ready, sem("qk_lo_ready")
    s_ready, s_taken, p_ready, a_ready = sem("s_ready"), sem("s_taken"), sem("p_ready"), sem("a_ready")
    tr_ready, tr_hi_ready, tr_taken = sem("tr_ready"), sem("tr_hi_ready"), sem("tr_taken")
    o_ready, o_taken = sem("o_ready"), sem("o_taken")
    o_ms_ready, o_rstd_ready, o_normed = sem("o_ms_ready"), sem("o_rstd_ready"), sem("o_normed")
    og_ready, og_stored = sem("og_ready"), t.og_stored
    inv_ready, ratio_ready, bias_step, iota_ready = sem("inv_ready"), sem("ratio_ready"), sem("bias_step"), sem("iota_ready")

    def windows(eng, window):
        window(0, 0)
        window(1, 1)
        with eng.Fori(1, H // 2 - 1) as pair:
            window(2 * pair, 0)
            window(2 * pair + 1, 1)
        window(H - 2, 0)
        window(H - 1, 1)
        window(H, 0)

    def has(h, what):
        if not isinstance(h, int):
            return True
        return {"last": h > 0, "own": h < H, "next": h < H - 1, "second": h < H - 2}[what]

    ctx = ExitStack()
    with ctx:
        s_ps = [ctx.enter_context(nc.psum_tensor(f"s_ps{i}", [P, S], F32)) for i in range(2)]
        tr_ps = [ctx.enter_context(nc.psum_tensor(f"tr_ps{i}", [P, 512], F32)) for i in range(2)]
        o_ps = [ctx.enter_context(nc.psum_tensor(f"o_ps{i}", [P, 2 * DV], F32)) for i in range(2)]
        block = ctx.enter_context(nc.Block())

        def lag(h, s, back):
            place = s - back
            if place >= 0:
                return has(h, "own"), h, place
            return has(h, "last"), h - 1, place + NT

        @block.sync
        def _(sp):
            def load_qk(h):
                after(sp, qk_hi_ready, 4 * h)
                after(sp, qk_lo_ready, 4 * h)
                load_head_qk(nc, sp, t, u_dram, h)

            def load_v(h, transposed):
                after(sp, tr_ready, transposed)
                load_head_v(nc, sp, t, u_dram, h)

            for b in range(2):
                sp.wait_ge(t.u_stored[b], 16 * CHUNKS)
            load_qk(1)
            load_v(1, made(-1, PROLOGUE, 4))

            def window(h, par):
                if has(h, "last"):
                    after(sp, og_ready, 4 * (h - 1))
                    sp.dma_start(gate[:], u_dram[bass.ds(2 * (h - 1) + G_BLOCK0, 2)].rearrange("b p s -> p b s")).then_inc(g_loaded, 16)

                def store(n):
                    if has(h, "last"):
                        sp.wait_ge(og_ready, 4 * (h - 1) + (2 * n + 2))
                        sp.dma_start(og_dram[1 - n][bass.ds(2 * (h - 1), 2)].rearrange("d p s -> p d s"), og_out[:]).then_inc(og_stored, 16)

                store(0)
                if has(h, "second"):
                    load_qk(h + 2)
                    groups = window_groups(h)
                    load_v(h + 2, made(h, groups, max(n for n, g in enumerate(groups) if g[0] == "v") + 1))
                if isinstance(h, int) and h == H - 1:
                    sp.wait_ge(s_ready, 16 * h)
                    sp.wait_ge(qk_hi_ready, 4 * H)
                    sp.wait_ge(qk_lo_ready, 4 * H)
                    sp.wait_ge(og_stored, 16 * OG_AHEAD)
                    sp.wait_ge(o_ready, 8 * h)
                    for k in range(4):
                        load_out_w(sp, t, A, 0, k)
                    for k in range(OG_AHEAD):
                        load_og(sp, t, og_dram, k)
                store(1)

            windows(sp, window)

        @block.gpsimd
        def _(pool):
            nc.gpsimd.memset(one_in_dv[:], 1.0 / DV).then_inc(consts_set, 1)
            nc.gpsimd.memset(eps[:], EPS).then_inc(consts_set, 1)
            pool.wait_ge(consts_set, 2)
            pool.wait_ge(t.u_stored[1], 16 * CHUNKS)
            nc.gpsimd.iota(bias[1][:], pattern=[[-1, S]], base=S - P, channel_multiplier=1,
                           allow_small_or_imprecise_dtypes=True).then_inc(iota_ready, 1)
            pool.wait_ge(iota_ready, 2)
            nc.gpsimd.affine_select(out=bias[1][:], in_=bias[1][:], compare_op=ALU.is_ge, fill=MASKED, base=S - P,
                                    pattern=[[-1, S]], channel_multiplier=1).then_inc(iota_ready, 1)

            def split_lo(h, par, maps):
                for j in maps:
                    pool.wait_ge(qk_hi_ready, 4 * h + (j + 1))
                    nc.gpsimd.tensor_tensor(qk_lo[par][:, j, :], qk_raw[:, j, :], qk_hi[par][:, j, :].bitcast(F32), ALU.subtract).then_inc(qk_lo_ready, 1)

            def norm(h, par, half):
                place = 4 * (2 - half)
                n = 2 * h + (2 - half)
                four = slice(4 * half, 4 * half + 4)
                pool.wait_ge(o_taken, 8 * h + place)
                nc.gpsimd.tensor_tensor(o_ssq[par][:, four], o_ssq[par][:, four], one_in_dv[:, four], ALU.mult).then_inc(o_ms_ready, 1)
                pool.wait_ge(o_ms_ready, 2 * n - 1)
                nc.gpsimd.tensor_tensor(o_ssq[par][:, four], o_ssq[par][:, four], eps[:, four], ALU.add).then_inc(o_ms_ready, 1)
                pool.wait_ge(o_ms_ready, 2 * n)
                after(pool, o_normed, n - 1)
                nc.gpsimd.tensor_tensor(o_rstd[:, four], o_ssq[par][:, four], t.minus_half[:, four], ALU.pow).then_inc(o_rstd_ready, 1)
                pool.wait_ge(o_rstd_ready, n)
                nc.gpsimd.tensor_tensor(o[par][:, four, :], o[par][:, four, :],
                                        o_rstd[:, four].rearrange("p (n o) -> p n o", o=1).broadcast_to((P, 4, DV)), ALU.mult).then_inc(o_normed, 1)

            def window(h, par):
                if has(h, "next"):
                    split_lo(h + 1, 1 - par, (0, 1))
                if has(h, "last"):
                    norm(h - 1, 1 - par, 0)
                if has(h, "next"):
                    split_lo(h + 1, 1 - par, (2, 3))
                if has(h, "own"):
                    norm(h, par, 1)

            windows(pool, window)

        @block.scalar
        def _(act):
            def split_qk(h, par, j):
                act.wait_ge(qk_loaded, 32 * (h + 1))
                after(act, s_ready, 16 * (h - 1))
                nc.scalar.activation(qk_hi[par][:, j, :], qk_raw[:, j, :], ACT.Copy).then_inc(qk_hi_ready, 1)

            def split_v(h, groups, place, g, par):
                act.wait_ge(tr_ready, made(h, groups, place) + 1)
                after(act, o_ready, 8 * h)
                nc.scalar.activation(v_hi[par][:, 2 * g:2 * g + 2, :], tr_ps[bank_of(h, place)][:].rearrange("p (i d) -> p i d", i=2),
                                     ACT.Copy).then_inc(tr_hi_ready, 1)

            for n, (_, _, g) in groups_at(-1, 0):
                split_v(-1, PROLOGUE, n, g, 0)

            def window(h, par):
                steps = range(NT) if has(h, "own") else range(4)
                groups = window_groups(h)
                for s in steps:
                    for n, (kind, _, g) in groups_at(h, s):
                        if kind == "a":
                            there, ah, place = lag(h, s, 2)
                            i = ORDER[place]
                            cols = slice(4 * g * P, min(4 * g + 4, i + 1) * P)
                            act.wait_ge(tr_ready, made(h, groups, n) + 1)
                            after(act, o_ready, 8 * h + s - 3)
                            nc.scalar.activation(aT_hi[s % 2][:, cols], tr_ps[bank_of(h, n)][:, 0:cols.stop - cols.start], ACT.Copy).then_inc(tr_hi_ready, 1)
                    if has(h, "own"):
                        i = ORDER[s]
                        width = (i + 1) * P
                        for m in range(2):
                            act.wait_ge(s_taken, 16 * h + (2 * s + m + 1))
                            after(act, a_ready, 8 * h + s - 1)
                            nc.scalar.activation(e[s % 2][m][:, 0:width], e[s % 2][m][:, 0:width], ACT.Exp, scale=-1.0,
                                                 bias=row_min[s % 2][:, m:m + 1], accum_out=row_sum[s % 2][:, m:m + 1]).then_inc(p_ready, 1)
                    there, oh, place = lag(h, s, 4)
                    if there:
                        op = par if place == s - 4 else 1 - par
                        i = ORDER[place]
                        act.wait_ge(o_ready, 8 * oh + place + 1)
                        if place == 0:
                            after(act, og_ready, 4 * (oh - 1))
                        after(act, o_taken, 8 * oh + place)
                        nc.scalar.activation(junk[:], o_ps[place % 2][:, 0:DV], ACT.Square, scale=row_inv[op][:, i, 0:1],
                                             accum_out=o_ssq[op][:, i:i + 1])
                        nc.scalar.activation(o[op][:, i, :], o_ps[place % 2][:, 0:DV], ACT.Copy, scale=row_inv[op][:, i, 0:1]).then_inc(o_taken, 1)
                    for n, (kind, _, g) in groups_at(h, s):
                        if kind == "v":
                            split_v(h, groups, n, g, 1 - par)
                    if has(h, "next") and s < 4:
                        split_qk(h + 1, 1 - par, s)

            windows(act, window)

        @block.vector
        def _(dve):
            def split_v(h, groups, place, g, par):
                dve.wait_ge(tr_hi_ready, split(h, groups, place) + 1)
                view = tr_ps[bank_of(h, place)][:].rearrange("p (i d) -> p i d", i=2)
                nc.vector.tensor_tensor(v_lo[par][:, 2 * g:2 * g + 2, :], view, v_hi[par][:, 2 * g:2 * g + 2, :].bitcast(F32), ALU.subtract).then_inc(tr_taken, 1)

            awaited = [dve.alloc_register(f"awaited{i}") for i in range(2)]
            for n, j in enumerate((0, 2, 1, 3)):
                dve.wait_ge(qk_hi_ready, 4)
                nc.vector.tensor_tensor(qk_lo[0][:, j, :], qk_raw[:, j, :], qk_hi[0][:, j, :].bitcast(F32), ALU.subtract).then_inc(qk_lo_ready, 1)
                if n == 1:
                    dve.wait_ge(iota_ready, 1)
                    nc.vector.tensor_scalar(bias[1][:], bias[1][:], -1.0 / SCALE, None, ALU.mult).then_inc(iota_ready, 1)
            for n, (_, _, g) in groups_at(-1, 0):
                split_v(-1, PROLOGUE, n, g, 0)
            dve.wait_ge(iota_ready, 3)

            def combine(h, par, place):
                q = place % 2
                i = ORDER[place]
                width = (i + 1) * P
                dve.wait_ge(p_ready, 16 * h + (2 * place + 2))
                after(dve, o_taken, 8 * (h - 1))
                nc.vector.reciprocal(row_inv[par][:, i, :], row_sum[q][:]).then_inc(inv_ready, 1)
                dve.wait_ge(inv_ready, 8 * h + (place + 1))
                nc.vector.scalar_tensor_tensor(out=ratio[:], in0=row_sum[q][:, 0:1], scalar=t.neg_lam[:], in1=row_inv[par][:, i, 1:2],
                                               op0=ALU.mult, op1=ALU.mult).then_inc(ratio_ready, 1)
                dve.wait_ge(ratio_ready, 8 * h + (place + 1))
                nc.vector.scalar_tensor_tensor(out=a[q][:, 0:width], in0=e[q][1][:, 0:width], scalar=ratio[:], in1=e[q][0][:, 0:width],
                                               op0=ALU.mult, op1=ALU.add).then_inc(a_ready, 1)

            def window(h, par):
                steps = range(NT)
                groups = window_groups(h)
                if isinstance(h, int) and h == 0:
                    dve.wait_ge(t.u_stored[0], 16 * CHUNKS)
                if has(h, "own"):
                    nc.vector.tensor_scalar(bias[par][:], bias[1 - par][:], 0.5, None, ALU.mult).then_inc(bias_step, 1)
                    dve.wait_ge(bias_step, h + 1)
                for s in steps:
                    if has(h, "own"):
                        i = ORDER[s]
                        width = (i + 1) * P
                        for m in range(2):
                            after_apart(dve, [(s_ready, 16 * h + (2 * s + m + 1)), (a_ready, 8 * h + (s - 1))], awaited)
                            nc.vector.tensor_tensor_reduce(out=e[s % 2][m][:, 0:width], in0=s_ps[m][:, 0:width], in1=bias[par][:, S - width:S],
                                                           scale=-SCALE, scalar=3.0e38, op0=ALU.add, op1=ALU.min,
                                                           accum_out=row_min[s % 2][:, m:m + 1]).then_inc(s_taken, 1)
                    there, ch, place = lag(h, s, 1)
                    if there:
                        combine(ch, par if place == s - 1 else 1 - par, place)
                    for n, (kind, _, g) in groups_at(h, s):
                        if kind == "a":
                            there, ah, place = lag(h, s, 2)
                            i = ORDER[place]
                            cols = slice(4 * g * P, min(4 * g + 4, i + 1) * P)
                            dve.wait_ge(tr_hi_ready, split(h, groups, n) + 1)
                            nc.vector.tensor_tensor(aT_lo[s % 2][:, cols], tr_ps[bank_of(h, n)][:, 0:cols.stop - cols.start],
                                                    aT_hi[s % 2][:, cols].bitcast(F32), ALU.subtract).then_inc(tr_taken, 1)
                        elif kind == "v":
                            split_v(h, groups, n, g, 1 - par)
                        else:
                            dve.wait_ge(tr_ready, made(h, groups, n) + 1)
                            dve.wait_ge(g_loaded, 16 * h)
                            after(dve, og_stored, 16 * (2 * (h - 1) + g // 2))
                            d, half = g % 2, 1 - g // 2
                            nc.vector.scalar_tensor_tensor(out=og_out[:, d, :], in0=tr_ps[bank_of(h, n)][:], scalar=t.subln_col[:, d:d + 1],
                                                           in1=gate[:, d, half * 512:(half + 1) * 512], op0=ALU.mult, op1=ALU.mult).then_inc(og_ready, 1)

            windows(dve, window)

        @block.tensor
        def _(pe):
            def transpose_v(h, groups, place, g):
                wait_bank(h, groups, place)
                bank = tr_ps[bank_of(h, place)]
                for i in range(2):
                    for d in range(2):
                        col = (2 * i + d) * P
                        last = nc.tensor.transpose(bank[:, col:col + P], v_raw[:, d, (2 * g + i) * P:(2 * g + i + 1) * P], t.ident[:])
                last.then_inc(tr_ready, 1)

            def wait_bank(h, groups, place):
                if place >= 1:
                    after_groups(h, groups[:place - 1])
                elif isinstance(h, int) and h <= -1:
                    return
                else:
                    after_previous(h)

            def after_groups(h, kinds):
                n_og = len([g for g in kinds if g[0] == "og"])
                after(pe, tr_taken, split(h, kinds, len(kinds)))
                if has(h, "last"):
                    after(pe, og_ready, (h - 1) * 4 + n_og)

            def after_previous(h):
                if isinstance(h, int) and h == 0:
                    after(pe, tr_taken, len(PROLOGUE) - 1)
                    return
                after(pe, tr_taken, split(h, [], 0) - (1 if isinstance(h, int) and h == 1 else 0))
                if not (isinstance(h, int) and h == 1):
                    after(pe, og_ready, (h - 1) * 4 - 1)

            pe.wait_ge(v_loaded, 16)
            for n, (_, _, g) in groups_at(-1, 0):
                transpose_v(-1, PROLOGUE, n, g)

            def scores(h, par, s):
                i = ORDER[s]
                width = (i + 1) * P
                for m in range(2):
                    after(pe, s_taken, 16 * h + (2 * s + m - 1))
                    for c0 in range(0, width, 512):
                        c1 = min(c0 + 512, width)
                        for j, (q, k) in enumerate(((qk_hi, qk_hi), (qk_hi, qk_lo), (qk_lo, qk_hi))):
                            last = nc.tensor.matmul(s_ps[m][:, c0:c1], q[par][:, m, i * P:(i + 1) * P], k[par][:, 2 + m, c0:c1],
                                                    start=(j == 0), stop=(j == 2))
                    last.then_inc(s_ready, 1)

            def products(h, par, place, window_h, window_s):
                q = place % 2
                i = ORDER[place]
                groups = window_groups(window_h)
                end = max(n for n, g in groups_at(window_h, window_s) if g[0] == "a") + 1
                pe.wait_ge(tr_taken, split(window_h, groups, end))
                after(pe, o_taken, 8 * h + (place - 1))
                for kt in range(i + 1):
                    rows = slice(kt * P, (kt + 1) * P)
                    for j, (x, v) in enumerate(((aT_hi, v_hi), (aT_hi, v_lo), (aT_lo, v_hi))):
                        last = nc.tensor.matmul(o_ps[q][:, 0:DV], x[q][:, rows], v[par][:, kt, :], start=(kt == 0 and j == 0), stop=(kt == i and j == 2))
                last.then_inc(o_ready, 1)

            def window(h, par):
                groups = window_groups(h)
                for s in range(NT):
                    for n, (kind, _, g) in groups_at(h, s):
                        if kind == "a":
                            there, ah, place = lag(h, s, 2)
                            i = ORDER[place]
                            pe.wait_ge(a_ready, 8 * ah + (place + 1))
                            wait_bank(h, groups, n)
                            for j in range(4 * g, min(4 * g + 4, i + 1)):
                                last = nc.tensor.transpose(tr_ps[bank_of(h, n)][:, (j - 4 * g) * P:(j - 4 * g + 1) * P],
                                                           a[place % 2][:, j * P:(j + 1) * P], t.ident[:])
                            last.then_inc(tr_ready, 1)
                    there, oh, place = lag(h, s, 3)
                    if there:
                        wh, ws = (h, s - 1) if s >= 1 else (h - 1, NT - 1)
                        products(oh, par if place == s - 3 else 1 - par, place, wh, ws)
                    for n, (kind, _, g) in groups_at(h, s):
                        if kind == "v":
                            pe.wait_ge(v_loaded, 16 * (h + 2))
                            transpose_v(h, groups, n, g)
                        elif kind == "og":
                            pe.wait_ge(o_normed, 2 * (h - 1) + g // 2 + 1)
                            wait_bank(h, groups, n)
                            d, half = g % 2, 1 - g // 2
                            for i in range(4):
                                last = nc.tensor.transpose(tr_ps[bank_of(h, n)][:, i * P:(i + 1) * P],
                                                           o[1 - par][:, 4 * half + i, d * P:(d + 1) * P], t.ident[:])
                            last.then_inc(tr_ready, 1)
                    if has(h, "own") and s < NT - 1:
                        scores(h, par, s + 1)
                    elif has(h, "next") and s == NT - 1:
                        pe.wait_ge(qk_lo_ready, 4 * (h + 2))
                        scores(h + 1, 1 - par, 0)

            pe.wait_ge(qk_lo_ready, 4)
            scores(0, 0, 0)
            windows(pe, window)


def output_projection(nc, sem, t, A, og_dram, out):
    og_raw, w_raw, og_loaded, wo_loaded = t.og_raw, t.wo_raw, t.og_loaded, t.wo_loaded
    put, at = region(nc, t.after_wo)
    z = put("z", [P, NT, D])
    og_hi = [put(f"og_hi{i}", [P, S], F32R) for i in range(2)]
    og_lo = [put(f"og_lo{i}", [P, S], F32R) for i in range(2)]
    w_hi = [put(f"wo_hi{i}", [P, NW], F32R) for i in range(2)]
    w_lo = [put(f"wo_lo{i}", [P, NW], F32R) for i in range(2)]
    gate_row = put("gate_row", [P, D])
    final_row = put("final_row", [P, D])
    gated = [put(f"gated{i}", [P, NW]) for i in range(4)]
    junk = put("z_squares", [P, D])
    assert at[0] <= t.free_at
    put, at = region(nc, t.after_og)
    z_ssq = put("z_ssq", [P, 2, NT])
    z_rstd = put("z_rstd", [P, NT])
    assert at[0] <= nc.sbuf_usable_end

    z_loaded, final_loaded = sem("z_loaded"), sem("final_loaded")
    og_hi_ready, og_lo_ready, wo_hi_ready, wo_lo_ready = sem("og_hi_ready"), sem("og_lo_ready"), sem("wo_hi_ready"), sem("wo_lo_ready")
    gate_ps_ready, gate_row_ready = sem("gate_ps_ready"), sem("gate_row_ready")
    step_done, y_ready, y_taken, z_added = sem("step_done"), sem("y_ready"), sem("y_taken"), sem("z_added")
    z_sum_ready = sem("z_sum_ready")
    z_ssq_ready, z_ms_ready, z_rstd_ready, z_normed, stored = sem("z_ssq_ready"), sem("z_ms_ready"), sem("z_rstd_ready"), sem("z_normed"), sem("out_stored")

    TOKENS = [slice(0, HALF), slice(HALF, S)]
    ctx = ExitStack()
    with ctx:
        y_ps = [ctx.enter_context(nc.psum_tensor(f"y_ps{i}", [P, NW], F32)) for i in range(NT)]
        block = ctx.enter_context(nc.Block())

        @block.sync
        def _(sp):
            def load_w(n, k):
                after(sp, wo_lo_ready, KT * n + (k - 3))
                load_out_w(sp, t, A, n, k)

            for k in range(4, KT):
                load_w(0, k)
                if k >= OG_AHEAD:
                    sp.wait_ge(t.og_stored, 16 * 2 * (k // 2 + 1))
                    load_og(sp, t, og_dram, k)
            for m in range(NT):
                sp.dma_start(z[:, m, :], A["x"][0, m * P:(m + 1) * P, :]).then_inc(z_loaded, 16)
            sp.dma_start(final_row[:], A["final_g"].rearrange("(o n) -> o n", o=1).broadcast_to((P, D))).then_inc(final_loaded, 16)
            with sp.Fori(1, OUT_N) as n:
                for k in range(KT):
                    load_w(n, k)
            for k in range(KT):
                after(sp, wo_lo_ready, KT * OUT_N + (k - 3))
                load_out_w(sp, t, A, OUT_N - 1, k)
            for m in range(NT):
                sp.wait_ge(z_normed, m + 1)
                sp.dma_start(out[0, m * P:(m + 1) * P, :], z[:, m, :]).then_inc(stored, 16)
            sp.wait_ge(stored, 16 * NT)

        @block.scalar
        def _(act):
            def split_hi(n, k, tokens=slice(0, S)):
                act.wait_ge(wo_loaded[k % 4], 64 * n + 16 * (k // 4 + 1))
                after(act, step_done, KT * n + (k - 1))
                nc.scalar.activation(w_hi[k % 2][:], w_raw[k % 4][:], ACT.Copy).then_inc(wo_hi_ready, 1)
                act.wait_ge(og_loaded[k], 32)
                nc.scalar.activation(og_hi[k % 2][:, tokens], og_raw[:, k, tokens], ACT.Copy).then_inc(og_hi_ready, 1)

            split_hi(0, 0)
            for n in range(OUT_N):
                act.wait_ge(gate_ps_ready, n + 1)
                nc.scalar.activation(gate_row[:, n * NW:(n + 1) * NW], y_ps[OUT_N + n][:], ACT.Copy).then_inc(gate_row_ready, 1)
            for k in range(1, KT):
                split_hi(0, k)
            with act.Fori(1, OUT_N - 1) as n:
                for k in range(KT):
                    split_hi(n, k)

            def square(m, part, cols):
                act.wait_ge(z_added, NT * (OUT_N - 2 + part) + m + 1)
                after(act, z_ssq_ready, squared[0])
                nc.scalar.activation(junk[:, cols], z[:, m, cols], ACT.Square, accum_out=z_ssq[:, part, m:m + 1]).then_inc(z_ssq_ready, 1)
                squared[0] += 1

            squared = [0]
            for k in range(KT):
                split_hi(OUT_N - 1, k, TOKENS[0])
                if k % 2 == 1:
                    square(k // 2, 0, slice(0, NW * (OUT_N - 1)))
            for k in range(KT):
                split_hi(OUT_N, k, TOKENS[1])
                if NT // 2 <= k < NT:
                    square(k - NT // 2, 1, slice(NW * (OUT_N - 1), D))
            for m in range(NT // 2, NT):
                square(m, 1, slice(NW * (OUT_N - 1), D))

        @block.vector
        def _(dve):
            def split_lo(n, k, tokens=slice(0, S)):
                dve.wait_ge(wo_hi_ready, KT * n + (k + 1))
                nc.vector.tensor_tensor(w_lo[k % 2][:], w_raw[k % 4][:], w_hi[k % 2][:].bitcast(F32), ALU.subtract).then_inc(wo_lo_ready, 1)
                dve.wait_ge(og_hi_ready, KT * n + (k + 1))
                nc.vector.tensor_tensor(og_lo[k % 2][:, tokens], og_raw[:, k, tokens], og_hi[k % 2][:, tokens].bitcast(F32), ALU.subtract).then_inc(og_lo_ready, 1)

            def take(n):
                for m in range(NT):
                    if m < NT - 1:
                        dve.wait_ge(y_ready, (NT - 1) * n + (m + 1))
                    else:
                        dve.wait_ge(step_done, KT * (n + 1))
                    after(dve, z_added, NT * n + (m - 3))
                    nc.vector.tensor_tensor(gated[m % 4][:], y_ps[m][:], gate_row[:, bass.ds(n * NW, NW)], ALU.mult).then_inc(y_taken, 1)

            for k in range(KT):
                split_lo(0, k)
            dve.wait_ge(gate_row_ready, OUT_N)

            def chunk(n):
                split_lo(n, 0)
                split_lo(n, 1)
                take(n - 1)
                for k in range(2, KT):
                    split_lo(n, k)

            def take_last(m):
                half, i = m // (NT // 2), m % (NT // 2)
                if i < NT // 2 - 1:
                    dve.wait_ge(y_ready, (NT - 1) * (OUT_N - 1) + (NT // 2 - 1) * half + (i + 1))
                else:
                    dve.wait_ge(step_done, KT * (OUT_N + half))
                after(dve, z_added, NT * (OUT_N - 1) + (m - 3))
                nc.vector.tensor_tensor(gated[m % 4][:], y_ps[m][:], gate_row[:, D - NW:D], ALU.mult).then_inc(y_taken, 1)

            def finish(m):
                dve.wait_ge(z_rstd_ready, m + 1)
                nc.vector.scalar_tensor_tensor(out=z[:, m, :], in0=z[:, m, :], scalar=z_rstd[:, m:m + 1], in1=final_row[:],
                                               op0=ALU.mult, op1=ALU.mult).then_inc(z_normed, 1)

            chunk(1)
            with dve.Fori(2, OUT_N - 1) as n:
                chunk(n)
            split_lo(OUT_N - 1, 0, TOKENS[0])
            split_lo(OUT_N - 1, 1, TOKENS[0])
            take(OUT_N - 2)
            for k in range(2, KT):
                split_lo(OUT_N - 1, k, TOKENS[0])
            split_lo(OUT_N, 0, TOKENS[1])
            split_lo(OUT_N, 1, TOKENS[1])
            dve.wait_ge(final_loaded, 16)
            for m in range(NT // 2):
                take_last(m)
            for k in range(2, KT):
                split_lo(OUT_N, k, TOKENS[1])
                if k % 2 == 0 and NT - 2 <= k < NT - 2 + NT:
                    finish((k - NT + 2) // 2)
            for m in range(NT // 2, NT):
                take_last(m)
            for m in range(NT // 2, NT):
                finish(m)

        @block.gpsimd
        def _(pool):
            def add(n, m):
                pool.wait_ge(y_taken, NT * n + (m + 1))
                part = z[:, m, bass.ds(n * NW, NW)]
                nc.gpsimd.tensor_tensor(part, part, gated[m % 4][:], ALU.add).then_inc(z_added, 1)

            pool.wait_ge(z_loaded, 16 * NT)
            with pool.Fori(0, OUT_N - 1) as n:
                for m in range(NT):
                    add(n, m)
            def rstd(m):
                pool.wait_ge(z_ssq_ready, NT + m + 1)
                nc.gpsimd.tensor_tensor(z_rstd[:, m:m + 1], z_ssq[:, 0, m:m + 1], z_ssq[:, 1, m:m + 1], ALU.add).then_inc(z_sum_ready, 1)
                pool.wait_ge(z_sum_ready, m + 1)
                nc.gpsimd.tensor_scalar(z_rstd[:, m:m + 1], z_rstd[:, m:m + 1], 1.0 / D, EPS, ALU.mult, ALU.add).then_inc(z_ms_ready, 1)
                pool.wait_ge(z_ms_ready, m + 1)
                nc.gpsimd.tensor_tensor(z_rstd[:, m:m + 1], z_rstd[:, m:m + 1], t.minus_half[:, 0:1], ALU.pow).then_inc(z_rstd_ready, 1)

            for half in range(2):
                tiles = range(half * NT // 2, (half + 1) * NT // 2)
                for m in tiles:
                    add(OUT_N - 1, m)
                    if m > tiles[0]:
                        rstd(m - 1)
                rstd(tiles[-1])

        @block.tensor
        def _(pe):
            for n in range(OUT_N):
                nc.tensor.matmul(y_ps[OUT_N + n][:], t.ones[:], t.gate_acc[:, n * NW:(n + 1) * NW], start=True, stop=True).then_inc(gate_ps_ready, 1)

            def chunk(n, tiles=range(NT)):
                for k in range(KT):
                    pe.wait_ge(og_lo_ready, KT * n + (k + 1))
                    for m in tiles:
                        if k == 0:
                            if isinstance(n, int) and n == 0 and m >= OUT_N:
                                pe.wait_ge(gate_row_ready, m - OUT_N + 1)
                            taken = min(n, OUT_N - 1) if isinstance(n, int) else n
                            after(pe, y_taken, NT * taken + (m + 1 - NT))
                        rows = slice(m * P, (m + 1) * P)
                        for j, (x, w) in enumerate(((og_hi, w_hi), (og_hi, w_lo), (og_lo, w_hi))):
                            last = nc.tensor.matmul(y_ps[m][:], x[k % 2][:, rows], w[k % 2][:], start=(k == 0 and j == 0),
                                                    stop=(k == KT - 1 and j == 2))
                        if k == KT - 1 and m < tiles[-1]:
                            last.then_inc(y_ready, 1)
                    last.then_inc(step_done, 1)

            chunk(0)
            with pe.Fori(1, OUT_N - 1) as n:
                chunk(n)
            chunk(OUT_N - 1, range(NT // 2))
            chunk(OUT_N, range(NT // 2, NT))


class Shared:
    pass


def hybrid_diffattn_kernel(nc, A, out):
    u_dram = nc.dram_tensor("u_T", [64, P, S], F32, kind="Internal")
    og_dram = [nc.dram_tensor(f"og_T{half}", [KT, P, HALF], F32, kind="Internal") for half in range(2)]
    t = Shared()
    put, at = region(nc, SBUF_BASE)
    t.ident = put("ident", [P, P])
    t.ones = put("ones", [P, P])
    t.minus_half = put("minus_half", [P, NT])
    t.c_act = put("c_act", [P, KT])
    t.subln_col = put("subln_col", [P, 2])
    t.neg_lam = put("neg_lam", [P, 1])
    t.gate_acc = put("gate_acc", [P, D])
    t.hi_at = at[0]
    t.h_hi = put("h_hi", [P, KT, S], F32R)
    t.lo_at = at[0]
    t.h_lo = put("h_lo", [P, KT, S], F32R)
    t.free_at = at[0]
    t.xT = nc.alloc_sbuf_tensor_at("x_normed_T", [P, KT, S], F32, offset=t.hi_at)
    with ExitStack() as ctx:
        def sem(name):
            return ctx.enter_context(nc.semaphore(name))

        t.after_w = place_weights(nc, t)
        place_ahead(nc, sem, t)
        t.proj_ready, t.w_hi_ready, t.w_lo_ready = sem("proj_ready"), sem("w_hi_ready"), sem("w_lo_ready")
        with ExitStack() as banks:
            t.early_ps = [banks.enter_context(nc.psum_tensor(f"early_ps{i}", [P, S], F32)) for i in range(EARLY)]
            t.late_ps = banks.enter_context(nc.psum_tensor("late_ps", [P, S], F32))
            modulation_and_first_blocks(nc, sem, t, A)
            input_projection(nc, sem, t, A, u_dram)
        attention(nc, sem, t, A, u_dram, og_dram)
        output_projection(nc, sem, t, A, og_dram, out)


_INS = ["x", "c", "norm_g", "ada_w", "ada_b", "attn_w_in", "attn_w_out", "attn_lam_q1", "attn_lam_k1", "attn_lam_q2",
        "attn_lam_k2", "attn_subln_g", "final_g"]


def kernel(**inputs):
    import numpy as _np
    import concourse.bacc as _bacc
    from concourse import mybir as _mybir
    from concourse.bass_utils import run_bass_kernel_spmd as _run

    nc = _bacc.Bacc("TRN2", target_bir_lowering=False, num_devices=1)
    arrays, args = {}, {}
    for name in _INS:
        a = _np.ascontiguousarray(inputs[name])
        arrays[f"in_{name}_dram"] = a
        args[name] = nc.dram_tensor(f"in_{name}_dram", a.shape, _mybir.dt.from_np(a.dtype), kind="ExternalInput").ap()
    out = nc.dram_tensor("out_dram", (1, S, D), _mybir.dt.float32, kind="ExternalOutput").ap()
    hybrid_diffattn_kernel(nc, args, out)
    r = _run(nc, [arrays], core_ids=[0])
    return r.results[0]["out_dram"]
```
